# Optimizing a Trainium2 kernel written in Bass

```python
import math
import jax, jax.numpy as jnp
from jax import lax
import numpy as np
import jax
import jax.numpy as jnp

D_MODEL = 2048
BATCH = 1
SEQ = 256
DEPTH = 1

N_MIXERS = 2
N_HEADS = 16
HEAD_DIM = 128
N_KV_GROUPS = 4
HEADS_PER_GROUP = N_HEADS // N_KV_GROUPS
CMP_BLOCK = 32
CMP_STRIDE = 16
CMP_HIDDEN = 2 * HEAD_DIM
SEL_BLOCK = 64
SEL_TOPK = 16
WINDOW = 512
Q_BLOCK = 128
N_GATES = 3
KV_WIDTH = N_KV_GROUPS * HEAD_DIM
NSA_IN_COLS = N_HEADS * HEAD_DIM + 6 * KV_WIDTH + N_GATES * N_HEADS
REL_BUCKETS = 32
REL_MAX_DIST = 128
SSM_GROUP = 16
SSM_GROUPS = D_MODEL // SSM_GROUP
SSM_STATE = 64
D_FF = ((8 * D_MODEL + 2) // 3 + 255) // 256 * 256
N_NSA_LAYERS = (DEPTH + N_MIXERS - 1) // N_MIXERS
N_S5_LAYERS = DEPTH // N_MIXERS
RMS_EPS = 1e-6
NEG_INF = -1e30
FORCE_SCORE = 1e9


def rmsnorm(x, g):
    x32 = x.astype(jnp.float32)
    y = x32 * lax.rsqrt(jnp.mean(x32 * x32, axis=-1, keepdims=True) + RMS_EPS)
    return (y * g.astype(jnp.float32)).astype(x.dtype)

def rel_bucket(dist):
    n = jnp.maximum(dist, 0)
    max_exact = REL_BUCKETS // 2
    large = max_exact + (jnp.log(jnp.maximum(n, 1).astype(jnp.float32) / max_exact)
                         / math.log(REL_MAX_DIST / max_exact)
                         * (REL_BUCKETS - max_exact)).astype(jnp.int32)
    large = jnp.minimum(large, REL_BUCKETS - 1)
    return jnp.where(n < max_exact, n, large)

def masked_softmax(s, mask):
    s = jnp.where(mask, s.astype(jnp.float32), NEG_INF)
    p = jax.nn.softmax(s, axis=-1)
    return jnp.where(mask, p, 0.0)

def nsa_mixer(h, rel_bias, w_in, w_out, pos_k, w1_k, w2_k, pos_v, w1_v, w2_v):
    Bsz, S, _ = h.shape
    G, HPG, DH = N_KV_GROUPS, HEADS_PER_GROUP, HEAD_DIM
    proj = h @ w_in
    qe = N_HEADS * DH
    bounds = [qe + i * KV_WIDTH for i in range(7)]
    q, kc, vc, ks, vs, kw, vw, gl = jnp.split(proj, bounds, axis=-1)
    q = q.reshape(Bsz, S, G, HPG, DH) * (DH ** -0.5)
    kc, vc, ks, vs, kw, vw = [a.reshape(Bsz, S, G, DH) for a in (kc, vc, ks, vs, kw, vw)]
    gates = jax.nn.sigmoid(gl.astype(jnp.float32)).astype(h.dtype).reshape(Bsz, S, N_GATES, G, HPG)
    t = jnp.arange(S, dtype=jnp.int32)

    n_cmp = (S - CMP_BLOCK) // CMP_STRIDE + 1
    starts = jnp.arange(n_cmp, dtype=jnp.int32) * CMP_STRIDE
    gidx = starts[:, None] + jnp.arange(CMP_BLOCK, dtype=jnp.int32)[None, :]

    def compress(kv, pos, w1, w2):
        blk = kv[:, gidx] + pos[None, None, :, None, :]
        blk = jnp.moveaxis(blk, 3, 2).reshape(Bsz, n_cmp, G, CMP_BLOCK * DH)
        return jax.nn.gelu(blk @ w1) @ w2

    kcc = compress(kc, pos_k, w1_k, w2_k)
    vcc = compress(vc, pos_v, w1_v, w2_v)
    dist_c = t[:, None] - (starts + CMP_BLOCK - 1)[None, :]
    mask_c = dist_c >= 0
    bias_c = rel_bias[rel_bucket(dist_c)].transpose(2, 0, 1).reshape(G, HPG, S, n_cmp)
    s_c = jnp.einsum('btghd,bcgd->bghtc', q, kcc).astype(jnp.float32) + bias_c
    p_c = masked_softmax(s_c, mask_c)
    o_c = jnp.einsum('bghtc,bcgd->btghd', p_c.astype(vcc.dtype), vcc)

    imp = p_c.sum(axis=2)
    n_sel = S // SEL_BLOCK
    ratio = SEL_BLOCK // CMP_STRIDE
    lo = CMP_BLOCK // CMP_STRIDE - 1
    count = ratio + lo
    right = max(0, (count - 1) + ratio * n_sel - lo - n_cmp)
    imp_pad = jnp.pad(imp, ((0, 0), (0, 0), (0, 0), (lo, right)))
    imp_slc = sum(imp_pad[..., k:k + ratio * n_sel:ratio] for k in range(count))
    j = jnp.arange(n_sel, dtype=jnp.int32)
    t_blk = t // SEL_BLOCK
    forced = (j[None, :] == 0) | (j[None, :] == t_blk[:, None]) | (j[None, :] == t_blk[:, None] - 1)
    causal_blk = (j * SEL_BLOCK)[None, :] <= t[:, None]
    score = jnp.where(forced, FORCE_SCORE, imp_slc)
    score = jnp.where(causal_blk, score, NEG_INF)
    k_top = min(SEL_TOPK, n_sel)
    _, sel_idx = lax.top_k(score, k_top)

    ks_blocks = ks.reshape(Bsz, n_sel, SEL_BLOCK, G, DH).transpose(0, 3, 1, 2, 4)
    vs_blocks = vs.reshape(Bsz, n_sel, SEL_BLOCK, G, DH).transpose(0, 3, 1, 2, 4)
    nq = S // Q_BLOCK
    q_chunks = q.reshape(Bsz, nq, Q_BLOCK, G, HPG, DH).transpose(1, 0, 2, 3, 4, 5)
    idx_chunks = sel_idx.reshape(Bsz, G, nq, Q_BLOCK, k_top).transpose(2, 0, 1, 3, 4)
    t0s = jnp.arange(nq, dtype=jnp.int32) * Q_BLOCK
    table_g = rel_bias.T.reshape(G, HPG, REL_BUCKETS)
    bi = jnp.arange(Bsz)[:, None, None, None]
    gi = jnp.arange(G)[None, :, None, None]
    gi5 = jnp.arange(G)[None, :, None, None, None]
    hi5 = jnp.arange(HPG)[None, None, :, None, None]
    in_blk = jnp.arange(SEL_BLOCK, dtype=jnp.int32)

    def sel_chunk(args):
        qc, ic, t0 = args
        kg = ks_blocks[bi, gi, ic].reshape(Bsz, G, Q_BLOCK, k_top * SEL_BLOCK, DH)
        vg = vs_blocks[bi, gi, ic].reshape(Bsz, G, Q_BLOCK, k_top * SEL_BLOCK, DH)
        kpos = (ic[..., None] * SEL_BLOCK + in_blk).reshape(Bsz, G, Q_BLOCK, k_top * SEL_BLOCK)
        tq = t0 + jnp.arange(Q_BLOCK, dtype=jnp.int32)
        dist = tq[None, None, :, None] - kpos
        bias = table_g[gi5, hi5, rel_bucket(dist)[:, :, None]]
        s = jnp.einsum('bqghd,bgqkd->bghqk', qc, kg).astype(jnp.float32) + bias
        p = masked_softmax(s, (dist >= 0)[:, :, None])
        return jnp.einsum('bghqk,bgqkd->bqghd', p.astype(vg.dtype), vg)

    o_s = lax.map(sel_chunk, (q_chunks, idx_chunks, t0s))
    o_s = o_s.transpose(1, 0, 2, 3, 4, 5).reshape(Bsz, S, G, HPG, DH)

    nb = S // Q_BLOCK
    n_band = WINDOW // Q_BLOCK

    def band(kv):
        padded = jnp.pad(kv, ((0, 0), (WINDOW, 0), (0, 0), (0, 0))).reshape(Bsz, nb + n_band, Q_BLOCK, G, DH)
        return jnp.concatenate([padded[:, i:i + nb] for i in range(n_band + 1)], axis=2)

    kwb, vwb = band(kw), band(vw)
    qi = jnp.arange(Q_BLOCK, dtype=jnp.int32)
    ki = jnp.arange((n_band + 1) * Q_BLOCK, dtype=jnp.int32)
    dist_w = qi[:, None] + WINDOW - ki[None, :]
    key_abs = jnp.arange(nb, dtype=jnp.int32)[:, None] * Q_BLOCK - WINDOW + ki[None, :]
    mask_w = ((dist_w >= 0) & (dist_w < WINDOW))[None] & (key_abs >= 0)[:, None, :]
    bias_w = rel_bias[rel_bucket(dist_w)].transpose(2, 0, 1).reshape(G, HPG, Q_BLOCK, -1)
    qw = q.reshape(Bsz, nb, Q_BLOCK, G, HPG, DH)
    s_w = jnp.einsum('bjqghd,bjkgd->bjghqk', qw, kwb).astype(jnp.float32) + bias_w
    p_w = masked_softmax(s_w, mask_w[:, None, None])
    o_w = jnp.einsum('bjghqk,bjkgd->bjqghd', p_w.astype(vwb.dtype), vwb).reshape(Bsz, S, G, HPG, DH)

    o = (gates[:, :, 0, :, :, None] * o_c + gates[:, :, 1, :, :, None] * o_s
         + gates[:, :, 2, :, :, None] * o_w)
    return o.reshape(Bsz, S, N_HEADS * DH) @ w_out

def s5_mixer(h, A_re, A_im, log_dt, B_re, B_im, C_re, C_im, D_skip, w_glu):
    Bsz, S, D = h.shape
    f32 = jnp.float32
    A_re, A_im, log_dt = A_re.astype(f32), A_im.astype(f32), log_dt.astype(f32)
    B_re, B_im, C_re, C_im = B_re.astype(f32), B_im.astype(f32), C_re.astype(f32), C_im.astype(f32)
    u = h.astype(f32).reshape(Bsz, S, SSM_GROUPS, SSM_GROUP)
    dt = jnp.exp(log_dt)[:, None]
    decay = jnp.exp(A_re * dt)
    ab_re = decay * jnp.cos(A_im * dt)
    ab_im = decay * jnp.sin(A_im * dt)
    pr, pi_ = ab_re - 1.0, ab_im
    den = A_re * A_re + A_im * A_im
    cf_re = (pr * A_re + pi_ * A_im) / den
    cf_im = (pi_ * A_re - pr * A_im) / den
    bb_re = cf_re[..., None] * B_re - cf_im[..., None] * B_im
    bb_im = cf_re[..., None] * B_im + cf_im[..., None] * B_re
    bu_re = jnp.einsum('bsgc,gnc->bsgn', u, bb_re)
    bu_im = jnp.einsum('bsgc,gnc->bsgn', u, bb_im)
    a_re = jnp.broadcast_to(ab_re, bu_re.shape)
    a_im = jnp.broadcast_to(ab_im, bu_im.shape)

    def combine(e1, e2):
        a1r, a1i, b1r, b1i = e1
        a2r, a2i, b2r, b2i = e2
        return (a1r * a2r - a1i * a2i, a1r * a2i + a1i * a2r,
                a2r * b1r - a2i * b1i + b2r, a2r * b1i + a2i * b1r + b2i)

    _, _, x_re, x_im = lax.associative_scan(combine, (a_re, a_im, bu_re, bu_im), axis=1)
    y = (jnp.einsum('bsgn,gcn->bsgc', x_re, C_re) - jnp.einsum('bsgn,gcn->bsgc', x_im, C_im)
         + D_skip.astype(f32).reshape(SSM_GROUPS, SSM_GROUP) * u)
    y = jax.nn.gelu(y).reshape(Bsz, S, D).astype(h.dtype)
    z = y @ w_glu
    return z[..., :D] * jax.nn.sigmoid(z[..., D:])

def swiglu(h, w_in, w_out):
    z = h @ w_in
    a, b = z[..., :D_FF], z[..., D_FF:]
    return (jax.nn.silu(a) * b) @ w_out

def first_inputs(seed: int = 0) -> dict:
    key = jax.random.key(seed)
    ks = jax.random.split(key, 32)

    def nrm(k, shape, scale):
        return jax.random.normal(k, shape, jnp.float32) * scale

    D, H, DH, G, N, C = D_MODEL, N_HEADS, HEAD_DIM, SSM_GROUPS, SSM_STATE, SSM_GROUP
    n_idx = jnp.arange(N, dtype=jnp.float32)
    return {
        "x": nrm(ks[0], (BATCH, SEQ, D), 1.0),
        "rel_bias": nrm(ks[1], (REL_BUCKETS, H), 0.2),
        "mix_norm_g": 1.0 + nrm(ks[2], (DEPTH, D), 0.02),
        "ffn_norm_g": 1.0 + nrm(ks[3], (DEPTH, D), 0.02),
        "final_norm_g": 1.0 + nrm(ks[4], (D,), 0.02),
        "nsa_w_in": nrm(ks[5], (N_NSA_LAYERS, D, NSA_IN_COLS), D ** -0.5),
        "nsa_w_out": nrm(ks[6], (N_NSA_LAYERS, H * DH, D), (H * DH) ** -0.5),
        "cmp_pos_k": nrm(ks[7], (N_NSA_LAYERS, CMP_BLOCK, DH), 0.1),
        "cmp_w1_k": nrm(ks[8], (N_NSA_LAYERS, CMP_BLOCK * DH, CMP_HIDDEN), (CMP_BLOCK * DH) ** -0.5),
        "cmp_w2_k": nrm(ks[9], (N_NSA_LAYERS, CMP_HIDDEN, DH), CMP_HIDDEN ** -0.5),
        "cmp_pos_v": nrm(ks[10], (N_NSA_LAYERS, CMP_BLOCK, DH), 0.1),
        "cmp_w1_v": nrm(ks[11], (N_NSA_LAYERS, CMP_BLOCK * DH, CMP_HIDDEN), (CMP_BLOCK * DH) ** -0.5),
        "cmp_w2_v": nrm(ks[12], (N_NSA_LAYERS, CMP_HIDDEN, DH), CMP_HIDDEN ** -0.5),
        "s5_A_re": -0.5 + nrm(ks[13], (N_S5_LAYERS, G, N), 0.01),
        "s5_A_im": math.pi * n_idx + nrm(ks[14], (N_S5_LAYERS, G, N), 0.01),
        "s5_log_dt": jax.random.uniform(ks[15], (N_S5_LAYERS, G), jnp.float32,
                                        math.log(1e-3), math.log(1e-1)),
        "s5_B_re": nrm(ks[16], (N_S5_LAYERS, G, N, C), (2 * C) ** -0.5),
        "s5_B_im": nrm(ks[17], (N_S5_LAYERS, G, N, C), (2 * C) ** -0.5),
        "s5_C_re": nrm(ks[18], (N_S5_LAYERS, G, C, N), (2 * N) ** -0.5),
        "s5_C_im": nrm(ks[19], (N_S5_LAYERS, G, C, N), (2 * N) ** -0.5),
        "s5_D": nrm(ks[20], (N_S5_LAYERS, D), 1.0),
        "s5_w_glu": nrm(ks[21], (N_S5_LAYERS, D, 2 * D), D ** -0.5),
        "ffn_w_in": nrm(ks[22], (DEPTH, D, 2 * D_FF), D ** -0.5),
        "ffn_w_out": nrm(ks[23], (DEPTH, D_FF, D), D_FF ** -0.5),
    }

def first_block(x, rel_bias, mix_norm_g, ffn_norm_g, final_norm_g, nsa_w_in, nsa_w_out,
              cmp_pos_k, cmp_w1_k, cmp_w2_k, cmp_pos_v, cmp_w1_v, cmp_w2_v,
              s5_A_re, s5_A_im, s5_log_dt, s5_B_re, s5_B_im, s5_C_re, s5_C_im, s5_D, s5_w_glu,
              ffn_w_in, ffn_w_out):
    h = x
    for i in range(DEPTH):
        hn = rmsnorm(h, mix_norm_g[i])
        li = i // N_MIXERS
        if i % N_MIXERS == 0:
            h = h + nsa_mixer(hn, rel_bias, nsa_w_in[li], nsa_w_out[li],
                              cmp_pos_k[li], cmp_w1_k[li], cmp_w2_k[li],
                              cmp_pos_v[li], cmp_w1_v[li], cmp_w2_v[li])
        else:
            h = h + s5_mixer(hn, s5_A_re[li], s5_A_im[li], s5_log_dt[li], s5_B_re[li], s5_B_im[li],
                             s5_C_re[li], s5_C_im[li], s5_D[li], s5_w_glu[li])
        h = h + swiglu(rmsnorm(h, ffn_norm_g[i]), ffn_w_in[i], ffn_w_out[i])
    return rmsnorm(h, final_norm_g)


CHUNK = 64
MLSTM_HEADS = 8
MLSTM_WIDTH = D_MODEL
MLSTM_HEAD_DIM = MLSTM_WIDTH // MLSTM_HEADS
QK_CONV_WIDTH = 4
POOL_GROUPS = 4
POOL_WIDTH = D_MODEL // 2
POOL_GROUP_DIM = POOL_WIDTH // POOL_GROUPS
POOL_WINDOWS = (2, 4, 8, 16)
IN_SPLITS = (MLSTM_WIDTH, MLSTM_WIDTH, MLSTM_WIDTH, MLSTM_WIDTH, MLSTM_WIDTH,
             MLSTM_HEADS, MLSTM_HEADS, POOL_WIDTH, POOL_WIDTH, D_MODEL, D_MODEL)
IN_WIDTH = 5 * MLSTM_WIDTH + 2 * MLSTM_HEADS + 2 * POOL_WIDTH + 2 * D_MODEL


def _rmsnorm(x, w):
    xf = x.astype(jnp.float32)
    y = xf * lax.rsqrt(jnp.mean(xf * xf, axis=-1, keepdims=True) + RMS_EPS)
    return (y * w.astype(jnp.float32)).astype(x.dtype)

def _partition(t):
    parts, start = [], 0
    for width in IN_SPLITS:
        parts.append(t[..., start:start + width])
        start += width
    return parts

def _causal_depthwise_conv(x, w, b):
    c = x.shape[-1]
    y = lax.conv_general_dilated(
        x, w[:, None, :].astype(x.dtype), window_strides=(1,),
        padding=[(w.shape[0] - 1, 0)], dimension_numbers=('NWC', 'WIO', 'NWC'),
        feature_group_count=c)
    return y + b.astype(x.dtype)

def _to_chunks(t, nc):
    b = t.shape[0]
    t = t.reshape((b, nc, CHUNK) + t.shape[2:])
    t = jnp.moveaxis(t, 1, 0)
    return jnp.swapaxes(t, 2, 3)

def _mlstm_chunkwise(q, k, v, ig, lf):
    bsz, s, nh, d = q.shape
    nc = s // CHUNK
    causal = jnp.tril(jnp.ones((CHUNK, CHUNK), dtype=bool))
    xs = (_to_chunks(q, nc), _to_chunks(k, nc), _to_chunks(v, nc),
          _to_chunks(ig, nc), _to_chunks(lf, nc))

    def step(carry, inp):
        c_st, n_st, m_st = carry
        qc, kc, vc, ic, fc = inp
        b = jnp.cumsum(fc, axis=-1)
        log_d = b[..., :, None] - b[..., None, :] + ic[..., None, :]
        log_d = jnp.where(causal, log_d, -jnp.inf)
        log_inter = b + m_st[..., None]
        m_row = jnp.maximum(jnp.max(log_d, axis=-1), log_inter)
        p = jnp.exp(log_d - m_row[..., None]) * jnp.einsum('bhld,bhsd->bhls', qc, kc)
        w_inter = jnp.exp(log_inter - m_row)
        num = (jnp.einsum('bhls,bhsd->bhld', p, vc)
               + w_inter[..., None] * jnp.einsum('bhlk,bhkv->bhlv', qc, c_st))
        den = jnp.sum(p, axis=-1) + w_inter * jnp.einsum('bhlk,bhk->bhl', qc, n_st)
        h = num / jnp.maximum(jnp.abs(den), jnp.exp(-m_row))[..., None]
        g = b[..., -1]
        log_w = g[..., None] - b + ic
        m_new = jnp.maximum(g + m_st, jnp.max(log_w, axis=-1))
        decay = jnp.exp(g + m_st - m_new)
        w = jnp.exp(log_w - m_new[..., None])
        c_new = decay[..., None, None] * c_st + jnp.einsum('bhs,bhsk,bhsv->bhkv', w, kc, vc)
        n_new = decay[..., None] * n_st + jnp.einsum('bhs,bhsk->bhk', w, kc)
        return (c_new, n_new, m_new), h

    init = (jnp.zeros((bsz, nh, d, d), jnp.float32),
            jnp.zeros((bsz, nh, d), jnp.float32),
            jnp.zeros((bsz, nh), jnp.float32))
    _, hs = lax.scan(step, init, xs)
    hs = jnp.moveaxis(jnp.swapaxes(hs, 2, 3), 0, 1)
    return hs.reshape(bsz, s, nh, d)

def _multiscale_pool(u):
    bsz, s, _ = u.shape
    uf = u.astype(jnp.float32).reshape(bsz, s, POOL_GROUPS, POOL_GROUP_DIM)
    cs = jnp.concatenate(
        [jnp.zeros((bsz, 1, POOL_GROUPS, POOL_GROUP_DIM), jnp.float32),
         jnp.cumsum(uf, axis=1)], axis=1)
    t = jnp.arange(1, s + 1)[:, None]
    win = jnp.array(POOL_WINDOWS, dtype=jnp.int32)[None, :]
    lo = jnp.maximum(t - win, 0)
    grp = jnp.arange(POOL_GROUPS)[None, :]
    window_sum = cs[:, 1:] - cs[:, lo, grp]
    count = (t - lo).astype(jnp.float32)
    return window_sum / count[..., None] - uf

def second_inputs(seed: int = 0) -> dict:
    key = jax.random.key(seed)
    ks = jax.random.split(key, 16)
    f32 = jnp.float32
    nrm = lambda k, shape, scale: (jax.random.normal(k, shape, f32) * scale)
    x = jax.random.normal(ks[0], (BATCH, SEQ, D_MODEL), f32)
    norm_pre_w = 1.0 + nrm(ks[1], (DEPTH, D_MODEL), 0.05)
    w_in = nrm(ks[2], (DEPTH, D_MODEL, IN_WIDTH), D_MODEL ** -0.5)
    mlstm_i_bias = nrm(ks[3], (DEPTH, MLSTM_HEADS), 0.1)
    mlstm_f_bias = (jnp.linspace(3.0, 6.0, MLSTM_HEADS, dtype=f32)[None, :]
                    + nrm(ks[4], (DEPTH, MLSTM_HEADS), 0.1))
    qk_conv_w = nrm(ks[5], (DEPTH, QK_CONV_WIDTH, 2 * MLSTM_WIDTH), QK_CONV_WIDTH ** -0.5)
    qk_conv_b = nrm(ks[6], (DEPTH, 2 * MLSTM_WIDTH), 0.01)
    mlstm_norm_w = 1.0 + nrm(ks[7], (DEPTH, MLSTM_WIDTH), 0.05)
    pool_w = nrm(ks[8], (DEPTH, POOL_GROUPS, POOL_GROUP_DIM, POOL_GROUP_DIM), POOL_GROUP_DIM ** -0.5)
    pool_scale = 1.0 + nrm(ks[9], (DEPTH, POOL_WIDTH), 0.1)
    w_proj_mlstm = nrm(ks[10], (DEPTH, MLSTM_WIDTH, D_MODEL), MLSTM_WIDTH ** -0.5)
    w_proj_pool = nrm(ks[11], (DEPTH, POOL_WIDTH, D_MODEL), POOL_WIDTH ** -0.5)
    w_out = nrm(ks[12], (DEPTH, D_MODEL, D_MODEL), D_MODEL ** -0.5)
    norm_post_w = 1.0 + nrm(ks[13], (DEPTH, D_MODEL), 0.05)
    return {'x': x, 'norm_pre_w': norm_pre_w, 'w_in': w_in,
            'mlstm_i_bias': mlstm_i_bias, 'mlstm_f_bias': mlstm_f_bias,
            'qk_conv_w': qk_conv_w, 'qk_conv_b': qk_conv_b,
            'mlstm_norm_w': mlstm_norm_w, 'pool_w': pool_w, 'pool_scale': pool_scale,
            'w_proj_mlstm': w_proj_mlstm, 'w_proj_pool': w_proj_pool,
            'w_out': w_out, 'norm_post_w': norm_post_w}

def second_block(x, norm_pre_w, w_in, mlstm_i_bias, mlstm_f_bias, qk_conv_w, qk_conv_b,
              mlstm_norm_w, pool_w, pool_scale, w_proj_mlstm, w_proj_pool, w_out,
              norm_post_w):
    bsz, s, _ = x.shape
    f32 = jnp.float32
    for l in range(DEPTH):
        h = _rmsnorm(x, norm_pre_w[l])
        proj = jnp.einsum('bsd,de->bse', h, w_in[l])
        (q, k, v, o_g, z_a, i_pre, f_pre, u_b, z_b, g_a, g_b) = _partition(proj)

        qk = jax.nn.silu(_causal_depthwise_conv(jnp.concatenate([q, k], axis=-1),
                                                qk_conv_w[l], qk_conv_b[l]))
        q = qk[..., :MLSTM_WIDTH].astype(f32).reshape(bsz, s, MLSTM_HEADS, MLSTM_HEAD_DIM)
        k = qk[..., MLSTM_WIDTH:].astype(f32).reshape(bsz, s, MLSTM_HEADS, MLSTM_HEAD_DIM)
        v = v.astype(f32).reshape(bsz, s, MLSTM_HEADS, MLSTM_HEAD_DIM)
        q = q * (MLSTM_HEAD_DIM ** -0.5)
        log_i = i_pre.astype(f32) + mlstm_i_bias[l].astype(f32)
        log_f = jax.nn.log_sigmoid(f_pre.astype(f32) + mlstm_f_bias[l].astype(f32))
        h_t = _mlstm_chunkwise(q, k, v, log_i, log_f)
        h_t = h_t * lax.rsqrt(jnp.mean(h_t * h_t, axis=-1, keepdims=True) + RMS_EPS)
        h_t = h_t * mlstm_norm_w[l].astype(f32).reshape(MLSTM_HEADS, MLSTM_HEAD_DIM)
        h_a = jax.nn.sigmoid(o_g.astype(f32)) * h_t.reshape(bsz, s, MLSTM_WIDTH)
        y_a = (h_a * jax.nn.silu(z_a.astype(f32))).astype(x.dtype)

        pooled = _multiscale_pool(u_b)
        mixed = jnp.einsum('bsgc,gcd->bsgd', pooled, pool_w[l].astype(f32))
        mixed = mixed.reshape(bsz, s, POOL_WIDTH) * pool_scale[l].astype(f32)
        y_b = (mixed * jax.nn.silu(z_b.astype(f32))).astype(x.dtype)

        br_a = jnp.einsum('bsc,cd->bsd', y_a, w_proj_mlstm[l])
        br_b = jnp.einsum('bsc,cd->bsd', y_b, w_proj_pool[l])
        merged = jax.nn.sigmoid(g_a) * br_a + jax.nn.sigmoid(g_b) * br_b
        out = jnp.einsum('bsd,de->bse', merged, w_out[l])
        x = x + _rmsnorm(out, norm_post_w[l])
    return x


def setup_inputs(seed=0):
    out = dict(first_inputs(seed))
    for name, value in second_inputs(seed + 1).items():
        if name != "x":
            out[name + "_2"] = value
    return out


def reference(
    x, rel_bias, mix_norm_g, ffn_norm_g, final_norm_g, nsa_w_in, nsa_w_out, cmp_pos_k, cmp_w1_k,
    cmp_w2_k, cmp_pos_v, cmp_w1_v, cmp_w2_v, s5_A_re, s5_A_im, s5_log_dt, s5_B_re, s5_B_im,
    s5_C_re, s5_C_im, s5_D, s5_w_glu, ffn_w_in, ffn_w_out, norm_pre_w_2, w_in_2, mlstm_i_bias_2,
    mlstm_f_bias_2, qk_conv_w_2, qk_conv_b_2, mlstm_norm_w_2, pool_w_2, pool_scale_2,
    w_proj_mlstm_2, w_proj_pool_2, w_out_2, norm_post_w_2,
):
    x = first_block(
        x, rel_bias, mix_norm_g, ffn_norm_g, final_norm_g, nsa_w_in, nsa_w_out, cmp_pos_k,
        cmp_w1_k, cmp_w2_k, cmp_pos_v, cmp_w1_v, cmp_w2_v, s5_A_re, s5_A_im, s5_log_dt, s5_B_re,
        s5_B_im, s5_C_re, s5_C_im, s5_D, s5_w_glu, ffn_w_in, ffn_w_out,
    )
    return second_block(
        x, norm_pre_w_2, w_in_2, mlstm_i_bias_2, mlstm_f_bias_2, qk_conv_w_2, qk_conv_b_2,
        mlstm_norm_w_2, pool_w_2, pool_scale_2, w_proj_mlstm_2, w_proj_pool_2, w_out_2,
        norm_post_w_2,
    )


_drawn_inputs = setup_inputs


def setup_inputs(seed=0):
    import zlib

    import numpy as np

    out = dict(_drawn_inputs(seed))
    spreads = {}
    factors = {'mix_norm_g': 3.259,
     'cmp_pos_k': 7.917,
     'mlstm_i_bias_2': 64.0,
     'qk_conv_b_2': 8.0,
     'mlstm_norm_w_2': 3.088,
     'ffn_norm_g': 4.253,
     'cmp_pos_v': 2.715}
    for name, (base, spread) in spreads.items():
        noise = np.random.default_rng([zlib.crc32(name.encode()), seed]).standard_normal(out[name].shape)
        drawn = base * np.exp(spread * noise) if base else spread * noise
        out[name] = jnp.asarray(drawn.astype(out[name].dtype))
    for name, factor in factors.items():
        out[name] = (out[name] * factor).astype(out[name].dtype)
    return out
```

```python
import math
from contextlib import ExitStack, contextmanager

import numpy as np

import concourse.bass as bass
from concourse import mybir

F32 = mybir.dt.float32
F32R = mybir.dt.float32r
ACT = mybir.ActivationFunctionType
ALU = mybir.AluOpType

P = 128
S = 256
D = 2048
TT = S // P
KT = D // P
HEADS, GROUPS, DH = 16, 4, 128
HPG = HEADS // GROUPS
CB, CS = 32, 16
NC = (S - CB) // CS + 1
BUCKETS, MAX_DIST = 32, 128
FF = 5632
FKT = FF // P
CH = 2 * DH
MH, MD = 8, 256
POOLS = (2, 4, 8, 16)
PG = 256
EPS = 1e-6
NEG = -1e30

BLK, FT = 512, 4
CC = 1024
NB = KT // 2
ND = FKT // 2
RING = 4
AHEAD = 3
NUP = FF // BLK
NML = 6 * NB
NMG = 3 * NB + NB // 2
C_KV = 0
C_G1 = C_KV + 6 * NB
C_CMP = C_G1 + 1
C_Q = C_CMP + 2 * NB
C_OUT = C_Q + 4 * NB
C_UP = C_OUT + 4 * NB
C_DOWN = C_UP + 2 * NUP * NB
C_ML = C_DOWN + 4 * ND
C_MG = C_ML + 1 + 4 * NML
C_WO = C_MG + 4 * NMG
CHUNKS = C_WO + 4 * NB
B_KV, B_G1, B_CMP, B_Q, B_OUT, B_UP = 0, 6, 7, 9, 13, 17
B_DOWN = B_UP + 2 * NUP
B_ML = B_DOWN + 4
B_MG = B_ML + 1 + 4 * 6
B_WO = B_MG + 4 * 4

TRI = P + S
O_SEL, O_CMP, O_WIN = 0, TRI, TRI + 32
PCOLS = O_WIN + TRI

Q_CONV, K_CONV, N_W, P_SC, P_W = 0, 20, 40, 44, 46
P_BAND = P_W + TT * PG
CUR = P_BAND + TT * S

MIX, FFN, FINAL, PRE, POST = range(5)


ATT_SLOTS = 12
ML_LINKS = 20


def real(gi, n):
    return n < HPG and (not isinstance(gi, int) or gi * HPG + n >= 0)


class Pos:

    def __init__(self, base, i=0, n=0):
        if isinstance(i, int):
            base, i, n = base + i * n, 0, 0
        assert n % RING == 0
        self.base, self.i, self.n = base, i, n

    def at(self, j):
        return self.base + j if self.n == 0 else self.i * self.n + (self.base + j)

    def slot(self, j):
        return (self.base + j) % RING

    def lap(self, j):
        lap = (self.base + j) // RING
        return lap if self.n == 0 else self.i * (self.n // RING) + lap

    def exists(self, j):
        return self.n != 0 or self.base + j < CHUNKS

    def after_first_lap(self, j):
        return self.n != 0 or self.base + j >= RING


class Chain:

    def __init__(self, engine, done):
        self.engine, self.done, self.start, self.k, self.i, self.per = engine, done, 0, 0, 0, 0

    def link(self, instruction):
        self.k += 1
        instruction.then_inc(self.done, 1)
        base = self.start + self.k
        self.engine.wait_ge(self.done, base if isinstance(self.i, int) else self.i * self.per + base)

    @contextmanager
    def loop(self, start, end, per):
        self.start, self.k = self.start + self.k, 0
        with self.engine.Fori(start, end) as i:
            self.i, self.per = i, per
            self.start -= start * per
            yield i
            assert self.k == per, (self.k, per)
        self.start, self.k, self.i, self.per = self.start + end * per, 0, 0, 0


def program(nc, d):
    ctx = ExitStack()

    def sb(name, shape, dt=F32, scope=ctx):
        return scope.enter_context(nc.sbuf_tensor(name, shape, dt))

    def sem(name):
        return ctx.enter_context(nc.semaphore(name))

    raw = [sb(f"raw{n}", [P, CC]) for n in range(RING)]
    w_hi = [sb(f"w_hi{n}", [P, CC], F32R) for n in range(RING)]
    w_lo = [sb(f"w_lo{n}", [P, CC], F32R) for n in range(RING)]
    x_hi = sb("x_hi", [P, KT, S], F32R)
    x_lo = sb("x_lo", [P, KT, S], F32R)
    h = sb("h", [P, KT, S])
    ident = sb("ident", [P, P])
    ones = sb("ones", [P, P])
    gains = sb("gains", [P, 5, KT])
    gain2 = sb("gain2", [P, KT])
    stat = sb("stat", [P, 2, S])
    sq = sb("sq", [P, FT, S])
    rms = sb("rms", [P, 5, S + TT])
    rtmp = sb("rtmp", [P, S + TT])

    with ExitStack() as s1:
        k_sw = sb("k_sw", [P, 2, GROUPS, S], scope=s1)
        v_sw = sb("v_sw", [P, 2, TT, GROUPS * DH], scope=s1)
        bias = sb("bias", [P, HEADS, S], scope=s1)
        bias_c = sb("bias_c", [P, HEADS, TT, NC], scope=s1)
        gate = sb("gate", [P, HEADS, 3, TT], scope=s1)
        g_sig = sb("g_sig", [P, TT, 48], scope=s1)
        q_t = sb("q_t", [P, HPG, S], scope=s1)
        k_g = sb("k_g", [P, 2, S], scope=s1)
        v_g = sb("v_g", [P, 2, TT, DH], scope=s1)
        k_c = sb("k_c", [P, GROUPS, NC], scope=s1)
        v_c = sb("v_c", [NC, GROUPS, DH], scope=s1)
        k_cg = sb("k_cg", [P, NC], scope=s1)
        v_cg = sb("v_cg", [NC, DH], scope=s1)
        w2 = sb("w2", [P, 2, 2, DH], scope=s1)
        pos = sb("pos", [P, 2, CB], scope=s1)
        flip = sb("flip", [P, P], scope=s1)
        valid = sb("valid", [P, TT], scope=s1)
        rel = sb("rel", [BUCKETS + 1, HEADS], scope=s1)
        hid_in = sb("hid_in", [P, 2, 2, GROUPS * NC], scope=s1)
        hid = sb("hid", [P, 2, 2, GROUPS * NC], scope=s1)
        with ExitStack() as s1a:
            onehot = sb("onehot", [BUCKETS + 1, NC, S], scope=s1a)
            ohd = sb("ohd", [BUCKETS + 1, 2 * S], scope=s1a)
            u_row = sb("u_row", [HEADS, 2 * S], scope=s1a)
        with ExitStack() as s1b:
            kv_c = sb("kv_c", [P, 2, GROUPS, S], scope=s1b)
            blk_in = sb("blk_in", [P, CB, GROUPS, NC], scope=s1b)
            blk_hi = sb("blk_hi", [P, 2, CB, GROUPS * NC], F32R, scope=s1b)
            blk_lo = sb("blk_lo", [P, 2, CB, GROUPS * NC], F32R, scope=s1b)
        with ExitStack() as s1c:
            o_hi = sb("o_hi", [P, HEADS, S], F32R, scope=s1c)
            o_lo = sb("o_lo", [P, HEADS, S], F32R, scope=s1c)
            prob = [sb(f"prob{n}", [P, PCOLS], scope=s1c) for n in range(2)]
            prob_t = sb("prob_t", [P, 2, TRI], scope=s1c)
            prob_ct = sb("prob_ct", [NC, S], scope=s1c)
            bias_g = sb("bias_g", [P, HPG, S], scope=s1c)
            bias_cg = sb("bias_cg", [P, HPG, TT, NC], scope=s1c)
            top = sb("top", [P, 3, TT], scope=s1c)
            ntop = sb("ntop", [P, 3, TT], scope=s1c)
            total = [sb(f"total{n}", [P, 3, TT], scope=s1c) for n in range(2)]
            share = [sb(f"share{n}", [P, 3, TT], scope=s1c) for n in range(2)]
    with ExitStack() as s2:
        f_hi = sb("f_hi", [P, FKT, S], F32R, scope=s2)
        f_lo = sb("f_lo", [P, FKT, S], F32R, scope=s2)
        f_a = sb("f_a", [P, FT, S], scope=s2)
        f_b = sb("f_b", [P, FT, S], scope=s2)
    with ExitStack() as s3:
        ya_hi = sb("ya_hi", [P, KT, S], F32R, scope=s3)
        ya_lo = sb("ya_lo", [P, KT, S], F32R, scope=s3)
        yb_hi = sb("yb_hi", [P, 2 * len(POOLS), S], F32R, scope=s3)
        yb_lo = sb("yb_lo", [P, 2 * len(POOLS), S], F32R, scope=s3)
        with ExitStack() as s3a:
            cur = sb("cur", [P, CUR], scope=s3a)
            decay = sb("decay", [P, MH, TRI], scope=s3a)
            emm = sb("emm", [P, TT, MH], scope=s3a)
            cq = sb("cq", [P, FT, S + 3], scope=s3a)
            qm = sb("qm", [P, FT, S], scope=s3a)
            km = sb("km", [P, FT, S], scope=s3a)
            vm = sb("vm", [P, TT, BLK], scope=s3a)
            oz = sb("oz", [P, FT, S], scope=s3a)
            t1 = sb("t1", [P, FT, S], scope=s3a)
            t2 = sb("t2", [P, FT, S], scope=s3a)
            pm = sb("pm", [P, TRI], scope=s3a)
            pm_t = sb("pm_t", [P, TRI], scope=s3a)
            den = sb("den", [P, 2, TT], scope=s3a)
            g_pre = sb("g_pre", [P, TT, 2 * MH], scope=s3a)
            g_bias = sb("g_bias", [P, 2 * MH], scope=s3a)
            g_t = sb("g_t", [P, 3, TT, MH], scope=s3a)
            g_max = sb("g_max", [P, MH, TT], scope=s3a)
            dec = sq[:, 0:3, :].rearrange("p a b -> p (a b)").rearrange("p (n c) -> p n c", n=2)
            hn = cq[:, :, 3:S + 3]
        with ExitStack() as s3b:
            m_hi = sb("m_hi", [P, KT, S], F32R, scope=s3b)
            m_lo = sb("m_lo", [P, KT, S], F32R, scope=s3b)
            m_a = sb("m_a", [P, FT, S], scope=s3b)
            m_b = sb("m_b", [P, FT, S], scope=s3b)
            m_t = sb("m_t", [P, FT, S], scope=s3b)
    with ExitStack() as s4:
        out_t = sb("out_t", [P, KT, S], scope=s4)
        y_t = sb("y_t", [P, KT, S], scope=s4)
    sel = oz[0:MH, :, :].rearrange("p a b -> p (a b)")
    causal = vm[:, 0, 0:TRI]
    tri = vm[:, 1, 0:P]
    g_row = vm[0:MH, 1, P:P + S]

    sets = [ctx.enter_context(nc.psum_tensor(f"set{n}", [P, 2 * BLK], F32)) for n in range(2)]
    m = [ctx.enter_context(nc.psum_tensor(f"misc{n}", [P, BLK], F32)) for n in range(4)]
    u_dram = nc.dram_tensor("u_dram", [HEADS, 2 * S], F32, kind="Internal").ap()

    raw_ready = [sem(f"raw_ready{n}") for n in range(RING)]
    hi_ready, lo_ready = sem("hi_ready"), sem("lo_ready")
    chunks_done = sem("chunks_done")
    taken = sem("taken")
    x_in = [sem(f"x_in{n}") for n in range(4)]
    gains_in, small_in = sem("gains_in"), sem("small_in")
    consts = sem("consts")
    dve_own, act_own, pool_own = sem("dve_own"), sem("act_own"), sem("pool_own")
    xh_ready, x_ready = sem("xh_ready"), sem("x_ready")
    hg_ready = sem("hg_ready")
    stats_ready, stats_sum = sem("stats_ready"), sem("stats_sum")
    var_ready, rms_ready = sem("var_ready"), sem("rms_ready")
    rel_done, u_ready, u_out, bias_in, bias_c_ready = (
        sem("rel_done"), sem("u_ready"), sem("u_out"), sem("bias_in"), sem("bias_c_ready"))
    flip_done, bias_ready = sem("flip_done"), sem("bias_ready")
    gates_sig = sem("gates_sig")
    blk_in_ready, blk_h_ready, blk_ready = sem("blk_in_ready"), sem("blk_h_ready"), sem("blk_ready")
    hid_ready, kvc_sum, kvc_ready = sem("hid_ready"), sem("kvc_sum"), sem("kvc_ready")
    q_ready, kg_ready, vg_ready, bg_ready = sem("q_ready"), sem("kg_ready"), sem("vg_ready"), sem("bg_ready")
    scores_done, masked, exps_done = sem("scores_done"), sem("masked"), sem("exps_done")
    share_ready, probs_ready = sem("share_ready"), sem("probs_ready")
    pt_done, pt_ready, o_done, o_ready = sem("pt_done"), sem("pt_ready"), sem("o_done"), sem("o_ready")
    up_sig, up_prod, fh_ready, f_ready = sem("up_sig"), sem("up_prod"), sem("fh_ready"), sem("f_ready")
    cur_in, cur_free, decay_in = sem("cur_in"), sem("cur_free"), sem("decay_in")
    z_sig, pool_done, pool_ready, mix_done = sem("z_sig"), sem("pool_done"), sem("pool_ready"), sem("mix_done")
    yb_made, ybh_ready, yb_ready = sem("yb_made"), sem("ybh_ready"), sem("yb_ready")
    conv_ready, conv_sig, qkv_ready = sem("conv_ready"), sem("conv_sig"), sem("qkv_ready")
    g2_pre, g2_log, g2_f, f_done, g_ready, g_row_done, g_row_ready, g_bc_done, decay_arg, decay_ready = (
        sem("g2_pre"), sem("g2_log"), sem("g2_f"), sem("f_done"), sem("g_ready"), sem("g_row_done"),
        sem("g_row_ready"), sem("g_bc_done"), sem("decay_arg"), sem("decay_ready"))
    ms_done, mp_ready, mpt_done, mpt_ready = sem("ms_done"), sem("mp_ready"), sem("mpt_done"), sem("mpt_ready")
    mh_done, mh_ready, mh_sq, mn_done = sem("mh_done"), sem("mh_ready"), sem("mh_sq"), sem("mn_done")
    dec_ready = sem("dec_ready")
    mn_var, mn_root, o_sig, zg_sig = sem("mn_var"), sem("mn_root"), sem("o_sig"), sem("zg_sig")
    ya_made, yah_ready, ya_ready = sem("ya_made"), sem("yah_ready"), sem("ya_ready")
    ga_sig, gb_sig, mg_made, mh2_ready, m_ready = (
        sem("ga_sig"), sem("gb_sig"), sem("mg_made"), sem("mh2_ready"), sem("m_ready"))
    y_ready, y_out = sem("y_ready"), sem("y_out")

    def row(n):
        return rms[:, n, 0:S]

    def rows(n, count=FT):
        return row(n).unsqueeze(1).to_broadcast([P, count, S])

    def col(n, t):
        return rms[:, n, S + t:S + t + 1]

    def flat(ap):
        return ap.rearrange("p a b -> p (a b)")

    block = ctx.enter_context(nc.Block())


    def ml_block(i, b):
        if isinstance(i, int) and i == 0 and b == 0:
            return Pos(C_ML), B_ML
        number = B_ML + 1 + b
        return Pos(C_ML + 1 + b * NB, i, NML), (number + 6 * i if isinstance(i, int) else i * 6 + number)

    def ml_set(i, b):
        return (B_ML + (0 if isinstance(i, int) and i == 0 and b == 0 else 1) + b) % 2

    @block.sync
    def _(sp):
        def load(c, slot):
            sp.dma_start(raw[slot][:, :], d["weights"][c]).then_inc(raw_ready[slot], 16)

        def load_x(n):
            sp.dma_start(h[:, 4 * n:4 * n + 4, :],
                         d["x"][4 * n:4 * n + 4].rearrange("k p s -> p k s")).then_inc(x_in[n], 16)

        load_x(0)
        load(0, 0)
        load_x(1)
        load(1, 1)
        load_x(2)
        load(2, 2)
        load_x(3)
        load(3, 3)
        with sp.Fori(1, CHUNKS // RING) as i:
            for n in range(RING):
                sp.wait_ge(lo_ready, i * RING + (n - RING + 1))
                load(i * RING + n, n)
        for c in range(CHUNKS // RING * RING, CHUNKS):
            sp.wait_ge(lo_ready, c - RING + 1)
            load(c, c % RING)
        for n in range(4):
            sp.wait_ge(y_ready, n + 1)
            sp.dma_start(d["out"][4 * n:4 * n + 4].rearrange("k p s -> p k s"),
                         y_t[:, 4 * n:4 * n + 4, :]).then_inc(y_out, 16)
        sp.wait_ge(y_out, 64)

    @block.gpsimd
    def _(pool):
        own = Chain(pool, pool_own)
        g = nc.gpsimd

        pool.dma_start(gains[:, :, :], d["gains"]).then_inc(gains_in, 16)
        for dst, name in ((rel[0:BUCKETS, :], "rel"), (onehot[:, :, :], "onehot"), (ohd[:, :], "ohd"),
                          (w2[:, :, :, :], "w2"), (pos[:, :, :], "pos"), (valid[:, :], "valid")):
            pool.dma_start(dst, d[name]).then_inc(small_in, 16)
        own.link(g.memset(rel[BUCKETS:BUCKETS + 1, :], 1.0))
        g.memset(ones[:, :], 1.0).then_inc(consts, 1)
        own.link(g.memset(ident[:, :], 0.0))
        g.affine_select(out=ident[:, :], in_=ident[:, :], compare_op=ALU.not_equal, fill=1.0, base=0,
                        pattern=[[-1, P]], channel_multiplier=1).then_inc(consts, 1)
        own.link(g.memset(flip[:, :], 0.0))
        g.affine_select(out=flip[:, :], in_=flip[:, :], compare_op=ALU.not_equal, fill=1.0, base=1 - P,
                        pattern=[[1, P]], channel_multiplier=1).then_inc(consts, 1)

        def squares(src, k, first):
            own.link(g.tensor_tensor(sq[:, :, :], src, src, ALU.mult))
            own.link(g.tensor_tensor(sq[:, 0:2, :], sq[:, 0:2, :], sq[:, 2:4, :], ALU.add))
            if first:
                last = g.tensor_tensor(stat[:, k, :], sq[:, 0, :], sq[:, 1, :], ALU.add)
            else:
                own.link(g.tensor_tensor(sq[:, 0, :], sq[:, 0, :], sq[:, 1, :], ALU.add))
                last = g.tensor_tensor(stat[:, k, :], stat[:, k, :], sq[:, 0, :], ALU.add)
            last.then_inc(stats_ready, 1)

        for n in range(4):
            pool.wait_ge(x_in[n], 16)
            if n:
                pool.wait_ge(stats_ready, n)
            squares(h[:, 4 * n:4 * n + 4, :], 0, n == 0)

        pool.wait_ge(u_ready, 1)
        pool.dma_start(u_dram, u_row[:, :]).then_inc(u_out, 16)
        pool.wait_ge(u_out, 16)
        pool.dma_start(bias[:, :, :], bass.AP(tensor=u_dram.tensor, offset=0,
                                              ap=[[1, P], [2 * S, HEADS], [1, S]])).then_inc(bias_in, 16)

        def group(gi, first):
            if not first:
                pool.wait_ge(scores_done, gi * HPG)
            for n in range(2):
                g.tensor_copy(k_g[:, n, :], k_sw[:, n, gi, :])
            g.tensor_copy(k_cg[:, :], k_c[:, gi, :]).then_inc(kg_ready, 1)
            if not first:
                pool.wait_ge(masked, gi * HPG)
            heads = bass.ds(gi * HPG, HPG)
            g.tensor_copy(bias_g[:, :, :], bias[:, heads, :])
            g.tensor_copy(bias_cg[:, :, :, :], bias_c[:, heads, :, :]).then_inc(bg_ready, 1)
            for n in range(HPG):
                if n == 1:
                    if not first:
                        pool.wait_ge(o_done, gi * HPG)
                    for b in range(2):
                        g.tensor_copy(v_g[:, b, :, :], v_sw[:, b, :, bass.ds(gi * DH, DH)])
                    g.tensor_copy(v_cg[:, :], v_c[:, gi, :]).then_inc(vg_ready, 1)
                pool.wait_ge(share_ready, gi * HPG + (n + 1))
                pr, sh = prob[n % 2], share[n % 2]
                for b, t, lo, w in ((1, 0, O_SEL, P), (1, 1, O_SEL + P, S), (0, 0, O_CMP, NC),
                                    (0, 1, O_CMP + 16, NC), (2, 0, O_WIN, P), (2, 1, O_WIN + P, S)):
                    last = g.tensor_tensor(pr[:, lo:lo + w], pr[:, lo:lo + w],
                                           sh[:, b, t:t + 1].to_broadcast([P, w]), ALU.mult)
                last.then_inc(probs_ready, 1)

        pool.wait_ge(taken, B_G1)
        pool.wait_ge(kvc_ready, 1)
        pool.wait_ge(bias_ready, 2)
        pool.wait_ge(bias_c_ready, 1)
        group(0, True)
        with pool.Fori(1, GROUPS) as gi:
            group(gi, False)

        pool.wait_ge(taken, B_OUT + 1)
        pool.wait_ge(rms_ready, 1)
        squares(h[:, 0:4, :], 0, True)
        with own.loop(1, 4, 3) as n:
            pool.wait_ge(taken, n + (B_OUT + 1))
            pool.wait_ge(stats_ready, n + 4)
            squares(h[:, bass.ds(n * 4, 4), :], 0, False)

        pool.wait_ge(rms_ready, 2)
        pool.wait_ge(hg_ready, 1)
        squares(h[:, 0:4, :], 0, True)
        pool.wait_ge(stats_ready, 9)
        squares(f_a[:, :, :], 1, True)
        with own.loop(1, 4, 6) as n:
            pool.wait_ge(hg_ready, n + 1)
            pool.wait_ge(stats_ready, n * 2 + 8)
            squares(h[:, bass.ds(n * 4, 4), :], 0, False)
            pool.wait_ge(stats_ready, n * 2 + 9)
            squares(f_a[:, :, :], 1, False)

        pool.wait_ge(chunks_done, C_ML)
        for dst, name in ((sel, "sel"), (causal, "causal"), (tri, "tri"), (g_bias[:, :], "g_bias")):
            pool.dma_start(dst, d[name]).then_inc(decay_in, 16)
        pool.dma_start(cur[:, :], d["cur"][0]).then_inc(cur_in, 16)
        pool.wait_ge(decay_ready, 2)
        g.tensor_copy(dec[:, :, :], decay[:, 0:2, :]).then_inc(dec_ready, 1)
        with pool.Fori(1, 4) as i:
            pool.wait_ge(cur_free, i)
            g.tensor_copy(dec[:, :, :], decay[:, bass.ds(i * 2, 2), :]).then_inc(dec_ready, 1)
            pool.dma_start(cur[:, :], d["cur"][i]).then_inc(cur_in, 16)

        pool.wait_ge(taken, B_WO + 1)
        pool.wait_ge(rms_ready, 4)
        squares(out_t[:, 0:4, :], 0, True)
        with own.loop(1, 4, 3) as n:
            pool.wait_ge(taken, n + (B_WO + 1))
            pool.wait_ge(stats_ready, n + 16)
            squares(out_t[:, bass.ds(n * 4, 4), :], 0, False)

    @block.scalar
    def _(act):
        own = Chain(act, act_own)
        a = nc.scalar.activation

        def split(at, j):
            if not at.exists(j):
                return
            act.wait_ge(raw_ready[at.slot(j)], (at.lap(j) + 1) * 16)
            if at.after_first_lap(j):
                act.wait_ge(chunks_done, at.at(j) - (RING - 1))
            a(w_hi[at.slot(j)][:, :], raw[at.slot(j)][:, :], ACT.Copy).then_inc(hi_ready, 1)

        def splits(at, count, extras=None):
            for j in range(count):
                split(at, j + AHEAD)
                if extras and j in extras:
                    extras[j]()

        def operand(kt, n, first):
            gain = gain2[:, kt] if n is None else gains[:, n, kt]
            a(x_hi[:, kt, :], h[:, kt, :], ACT.Copy, scale=gain).then_inc(xh_ready, 1)

        def root(n, count):
            act.wait_ge(var_ready, count)
            a(rms[:, n, :], rtmp[:, :], ACT.Sqrt).then_inc(rms_ready, 1)

        start = Pos(C_KV)
        act.wait_ge(gains_in, 16)
        for n in range(4):
            act.wait_ge(x_in[n], 16)
            for kt in range(4 * n, 4 * n + 4):
                operand(bass.ds(kt, 1), MIX, True)
            if n < AHEAD:
                split(start, n)

        def take_bias(half):
            act.wait_ge(flip_done, half + 1)
            for n in range(4):
                head = half * 8 + 2 * n
                last = a(bias[:, head:head + 2, :].rearrange("p a s -> p (a s)"), m[n][:, :], ACT.Copy)
            last.then_inc(bias_ready, 1)

        splits(Pos(C_KV), NB, {6: lambda: root(MIX, 1)})
        splits(Pos(C_KV + NB), NB, {2: lambda: take_bias(0), 5: lambda: take_bias(1)})
        for n in range(2):

            def blk_high(n=n):
                act.wait_ge(blk_in_ready, 2 * n + 2)
                a(blk_hi[:, n, :, :].rearrange("p l c -> p (l c)"),
                  blk_in[:, :, :, :].rearrange("p l g c -> p (l g c)"), ACT.Copy).then_inc(blk_h_ready, 1)

            splits(Pos(C_KV + 2 * NB, n, NB), NB, {2: blk_high})
        for n in range(2):
            splits(Pos(C_KV + 4 * NB, n, NB), NB)

        def gate_sigmoid():
            act.wait_ge(taken, B_G1 + 1)
            a(g_sig[:, :, :], g_sig[:, :, :], ACT.Sigmoid).then_inc(gates_sig, 1)

        splits(Pos(C_G1), 1)
        gate_sigmoid()
        for n in range(2):
            splits(Pos(C_CMP + n * NB), NB)
            act.wait_ge(taken, B_CMP + n + 1)
            a(hid[:, n, :, :], hid_in[:, n, :, :], ACT.Gelu_apprx_tanh).then_inc(hid_ready, 1)

        def exps(gi, n):
            act.wait_ge(masked, gi * HPG + (n + 1))
            pr = prob[n % 2]
            for b, t, lo, w in ((1, 0, O_SEL, P), (1, 1, O_SEL + P, S), (0, 0, O_CMP, NC),
                                (0, 1, O_CMP + 16, NC), (2, 0, O_WIN, P), (2, 1, O_WIN + P, S)):
                last = a(pr[:, lo:lo + w], pr[:, lo:lo + w], ACT.Exp, bias=ntop[:, b, t:t + 1],
                         accum_out=total[n % 2][:, b, t:t + 1])
            last.then_inc(exps_done, 1)

        def take_pt(gi, n):
            act.wait_ge(pt_done, gi * HPG + (n + 1))
            if real(gi, n - 1):
                act.wait_ge(o_done, gi * HPG + n)
            a(prob_t[:, 0, :], m[2][:, 0:TRI], ACT.Copy)
            a(prob_ct[:, 0:P], m[2][0:NC, TRI:BLK], ACT.Copy)
            a(prob_t[:, 1, :], m[3][:, 0:TRI], ACT.Copy)
            a(prob_ct[:, P:S], m[3][0:NC, TRI:BLK], ACT.Copy).then_inc(pt_ready, 1)

        def attention(gi, slot):
            n = slot // 2
            if slot % 2 == 0:
                if real(gi, n - 2):
                    take_pt(gi, n - 2)
                if real(gi, n - 1):
                    exps(gi, n - 1)

        def attentions(gi, slots=NB):
            return {s: lambda s=s: attention(gi, s) for s in range(slots)}

        splits(Pos(C_Q), NB)
        splits(Pos(C_Q + NB), NB, attentions(0))
        with act.Fori(1, GROUPS - 1) as gi:
            splits(Pos(C_Q + NB, gi, NB), NB, attentions(gi))

        def out_operand(n):
            for f in range(FT):
                act.wait_ge(taken, n + (B_OUT + 1))
                operand(bass.ds(n * FT + f, 1), FFN, False)

        splits(Pos(C_OUT), 2 * NB, attentions(3, ATT_SLOTS + 1) | {14: lambda: out_operand(0)})
        out_operand(1)
        with act.Fori(2, 4) as n:
            splits(Pos(C_OUT, n, NB), NB)
            out_operand(n)

        def up(i, first):
            splits(Pos(C_UP, i, 2 * NB), NB, {5: lambda: root(FFN, 2)} if first else None)
            act.wait_ge(taken, i * 2 + (B_UP + 1))
            a(f_b[:, :, :], f_a[:, :, :], ACT.Sigmoid).then_inc(up_sig, 1)
            splits(Pos(C_UP + NB, i, 2 * NB), NB)
            act.wait_ge(up_prod, i + 1)
            a(f_hi[:, bass.ds(i * FT, FT), :], f_b[:, :, :], ACT.Copy).then_inc(fh_ready, 1)

        up(0, True)
        with act.Fori(1, NUP) as i:
            up(i, False)

        with act.Fori(0, 2) as i:
            for b in range(2):
                splits(Pos(C_DOWN + b * ND, i, 2 * ND), ND)
                act.wait_ge(taken, i * 2 + (B_DOWN + b + 1))
                for f in range(FT):
                    operand(bass.ds(i * (2 * FT) + (b * FT + f), 1), None, False)

        def mlstm(i, first):
            e0 = {6: lambda: root(FINAL, 3)} if first else None
            splits(ml_block(i, 0)[0], NB, e0)
            if first:
                root(PRE, 4)
            act.wait_ge(taken, ml_block(i, 0)[1] + 1)
            a(t2[:, 0:2, :], t1[:, 2:4, :], ACT.Sigmoid).then_inc(z_sig, 1)
            if first:
                splits(Pos(C_ML + NB), 1)
                act.wait_ge(g2_pre, 1)
                own.link(a(g_t[:, 1, :, :], g_t[:, 0, :, :], ACT.Exp))
                a(g_t[:, 1, :, :], g_t[:, 1, :, :], ACT.Ln, bias=1.0).then_inc(g2_log, 1)

            def yb_high():
                act.wait_ge(yb_made, i + 1)
                a(yb_hi[:, bass.ds(i * 2, 2), :], t2[:, 2:4, :], ACT.Copy).then_inc(ybh_ready, 1)

            def conv_sigmoid(n):
                act.wait_ge(conv_ready, i * 2 + (n + 1))
                a(t2[:, :, :], t1[:, :, :], ACT.Sigmoid).then_inc(conv_sig, 1)

            def decays(n):
                act.wait_ge(decay_arg, 1)
                for k in range(n, n + MH // 2):
                    for t in range(TT):
                        part = decay[:, k, t * P:(t + 1) * P + t * P]
                        last = a(part, part, ACT.Exp, bias=g_max[:, k, t:t + 1])
                if n:
                    last = a(emm[:, :, :], emm[:, :, :], ACT.Exp)
                last.then_inc(decay_ready, 1)

            splits(ml_block(i, 1)[0], NB, {5: yb_high})
            conv_sigmoid(0)
            splits(ml_block(i, 2)[0], NB, {5: lambda: decays(0), 6: lambda: decays(MH // 2)} if first else None)
            conv_sigmoid(1)
            splits(ml_block(i, 3)[0], NB)

            def take_pmt(n):
                act.wait_ge(mpt_done, i * 2 + (n + 1))
                a(pm_t[:, :], m[1][:, 0:TRI], ACT.Copy).then_inc(mpt_ready, 1)

            def square(n):
                act.wait_ge(mh_ready, i * 2 + (n + 1))
                a(t2[:, 2 * n:2 * n + 2, :], hn[:, 2 * n:2 * n + 2, :], ACT.Square).then_inc(mh_sq, 1)

            def head_root(n):
                act.wait_ge(mn_var, i * 2 + (n + 1))
                a(t1[:, 2 + n, :], t1[:, n, :], ACT.Sqrt).then_inc(mn_root, 1)

            splits(ml_block(i, 4)[0], NB, {4: lambda: take_pmt(0), 6: lambda: square(0)})
            act.wait_ge(taken, ml_block(i, 4)[1] + 1)
            a(oz[:, :, :], t1[:, :, :], ACT.Sigmoid).then_inc(o_sig, 1)
            splits(ml_block(i, 5)[0], NB, {0: lambda: take_pmt(1), 2: lambda: square(1), 3: lambda: head_root(0),
                                           5: lambda: head_root(1)})
            act.wait_ge(taken, ml_block(i, 5)[1] + 1)
            a(t2[:, :, :], t1[:, :, :], ACT.Sigmoid).then_inc(zg_sig, 1)
            act.wait_ge(ya_made, i + 1)
            a(ya_hi[:, bass.ds(i * FT, FT), :], hn, ACT.Copy).then_inc(yah_ready, 1)

        mlstm(0, True)
        with act.Fori(1, 4) as i:
            mlstm(i, False)

        with act.Fori(0, 4) as i:
            splits(Pos(C_MG, i, NMG), NB)
            act.wait_ge(taken, i * 4 + (B_MG + 1))
            a(m_a[:, :, :], m_a[:, :, :], ACT.Sigmoid).then_inc(ga_sig, 1)
            splits(Pos(C_MG + NB, i, NMG), NB)
            act.wait_ge(taken, i * 4 + (B_MG + 2))
            a(m_b[:, :, :], m_b[:, :, :], ACT.Sigmoid).then_inc(gb_sig, 1)
            splits(Pos(C_MG + 2 * NB, i, NMG), NB)
            splits(Pos(C_MG + 3 * NB, i, NMG), NB // 2)
            act.wait_ge(mg_made, i + 1)
            a(m_hi[:, bass.ds(i * FT, FT), :], m_t[:, :, :], ACT.Copy).then_inc(mh2_ready, 1)

        with act.Fori(0, 3) as i:
            splits(Pos(C_WO, i, NB), NB)
        splits(Pos(C_WO, 3, NB), NB)
        root(POST, 5)

    @block.vector
    def _(dve):
        own = Chain(dve, dve_own)
        v = nc.vector
        tt, stt = v.tensor_tensor, v.scalar_tensor_tensor

        def split(at, j):
            if not at.exists(j):
                return
            dve.wait_ge(hi_ready, at.at(j) + 1)
            s = at.slot(j)
            tt(w_lo[s][:, :], raw[s][:, :], w_hi[s][:, :].bitcast(F32), ALU.subtract).then_inc(lo_ready, 1)

        def splits(at, count, extras=None):
            for j in range(count):
                split(at, j + AHEAD)
                if extras and j in extras:
                    extras[j]()
            dve.wait_ge(chunks_done, at.at(count))

        def psum(number):
            return sets[number % 2][:, :].rearrange("p (f s) -> p f s", f=FT)

        def operand(kt, n, count):
            gain = gain2[:, kt] if n is None else gains[:, n, kt]
            dve.wait_ge(xh_ready, count)
            stt(x_lo[:, kt, :], h[:, kt, :], gain, x_hi[:, kt, :].bitcast(F32),
                ALU.mult, ALU.subtract).then_inc(x_ready, 1)

        def variance(count, bank=0):
            dve.wait_ge(stats_sum, count)
            own.link(v.tensor_scalar(rtmp[:, :], m[bank][:, 0:S + TT], 1.0 / D, EPS, ALU.mult, ALU.add))
            v.reciprocal(rtmp[:, :], rtmp[:, :]).then_inc(var_ready, 1)

        start = Pos(C_KV)
        dve.wait_ge(gains_in, 16)
        tt(gain2[:, :], gains[:, FINAL, :], gains[:, PRE, :], ALU.mult)
        for n in range(4):
            for kt in range(4 * n, 4 * n + 4):
                operand(bass.ds(kt, 1), MIX, kt + 1)
            if n < AHEAD:
                split(start, n)

        dve.wait_ge(rel_done, 1)
        v.tensor_copy(u_row[:, :], m[3][0:HEADS, :]).then_inc(u_ready, 1)
        v.tensor_copy(bias_c[:, :, :, :],
                      m[2][:, 0:TT * NC * HEADS].rearrange("p (t c h) -> p h t c", t=TT, c=NC)).then_inc(bias_c_ready, 1)

        def take(number, dst, norm, scale=None):
            if scale is None:
                tt(dst, psum(number), rows(norm), ALU.mult).then_inc(taken, 1)
            else:
                stt(dst, psum(number), scale, rows(norm), ALU.mult, ALU.mult).then_inc(taken, 1)

        def take_tokens(number, dsts, norm, width=BLK):
            for t in range(TT):
                last = v.tensor_scalar(dsts[t], sets[number % 2][:, t * width:t * width + dsts[t].shape[-1]],
                                       col(norm, t), None, ALU.mult)
            last.then_inc(taken, 1)

        splits(Pos(C_KV), NB, {5: lambda: variance(1)})
        dve.wait_ge(rms_ready, 1)
        dve.wait_ge(u_out, 16)
        take(B_KV, kv_c[:, 0, :, :], MIX)
        splits(Pos(C_KV + NB), NB)
        take(B_KV + 1, kv_c[:, 1, :, :], MIX)
        for n in range(2):

            def blk_input(n=n):
                dve.wait_ge(taken, B_KV + n + 1)
                if n == 0:
                    dve.wait_ge(small_in, 96)
                for half in range(2):
                    src = kv_c[:, n, :, :].rearrange("p g (c l) -> p l g c", l=CS)[:, :, :, half:half + NC]
                    tt(blk_in[:, half * CS:(half + 1) * CS, :, :], src,
                       pos[:, n, half * CS:(half + 1) * CS].unsqueeze(2).unsqueeze(3)
                       .to_broadcast([P, CS, GROUPS, NC]), ALU.add).then_inc(blk_in_ready, 1)

            def blk_low(n=n):
                dve.wait_ge(blk_h_ready, n + 1)
                tt(blk_lo[:, n, :, :].rearrange("p l c -> p (l c)"),
                   blk_in[:, :, :, :].rearrange("p l g c -> p (l g c)"),
                   blk_hi[:, n, :, :].rearrange("p l c -> p (l c)").bitcast(F32),
                   ALU.subtract).then_inc(blk_ready, 1)

            splits(Pos(C_KV + (2 + n) * NB), NB, {1: blk_input, 3: blk_low})
            take(B_KV + 2 + n, k_sw[:, n, :, :], MIX)
        for n in range(2):
            splits(Pos(C_KV + (4 + n) * NB), NB)
            take_tokens(B_KV + 4 + n, [v_sw[:, n, t, :] for t in range(TT)], MIX)
        splits(Pos(C_G1), 1)
        for t in range(TT):
            last = v.tensor_scalar(g_sig[:, t, :], sets[B_G1 % 2][:, t * BLK:t * BLK + 48], col(MIX, t), None, ALU.mult)
        last.then_inc(taken, 1)

        def gates_out():
            dve.wait_ge(gates_sig, 1)
            for t in range(TT):
                own.link(v.tensor_copy(gate[:, :, :, t], g_sig[:, t, :].rearrange("p (b h) -> p h b", b=3)))
            own.link(tt(gate[:, :, 0, :], gate[:, :, 0, :], valid[:, :].unsqueeze(1).to_broadcast([P, HEADS, TT]), ALU.mult))

        for n in range(2):
            splits(Pos(C_CMP + n * NB), NB, {5: gates_out} if n == 0 else None)
            v.tensor_copy(hid_in[:, n, :, :],
                          sets[(B_CMP + n) % 2][:, :].rearrange("p (f c) -> p f c", f=2)[:, :, 0:GROUPS * NC]
                          ).then_inc(taken, 1)

        def compressed():
            dve.wait_ge(kvc_sum, 1)
            v.tensor_copy(k_c[:, :, :].rearrange("p g c -> p (g c)"), m[0][:, 0:GROUPS * NC])
            v.tensor_copy(v_c[:, :, :].rearrange("p g d -> p (g d)"), m[1][0:NC, :]).then_inc(kvc_ready, 1)

        def mask_scores(gi, n):
            head = gi * HPG + n
            if n == 0:
                dve.wait_ge(bg_ready, gi + 1)
            dve.wait_ge(scores_done, head + 1)
            if not (isinstance(gi, int) and gi * HPG + n < 2):
                dve.wait_ge(pt_done, head - 1)
            pr = prob[n % 2]
            pair = "p (t c) -> p t c"
            pr_c = pr[:, O_CMP:O_CMP + 32].rearrange(pair, t=TT)[:, :, 0:NC]
            tt(pr_c, m[0][:, TRI:TRI + 32].rearrange(pair, t=TT)[:, :, 0:NC], bias_cg[:, n, :, :], ALU.add)
            for b, t, o, src, add in (
                    (1, 0, O_SEL, m[0][:, 0:P], bias_g[:, n, P:S]),
                    (1, 1, O_SEL + P, m[0][:, P:TRI], bias_g[:, n, :]),
                    (2, 0, O_WIN, m[1][:, 0:P], bias_g[:, n, P:S]),
                    (2, 1, O_WIN + P, m[1][:, P:TRI], bias_g[:, n, :])):
                last = v.tensor_tensor_reduce(out=pr[:, o:o + (t + 1) * P], in0=src, in1=add, scale=1.0,
                                              scalar=-3e38, op0=ALU.add, op1=ALU.max, accum_out=top[:, b, t:t + 1])
            own.link(last)
            last = v.tensor_reduce(top[:, 0, :], pr_c, mybir.AxisListType.X, ALU.max)
            own.link(last)
            v.tensor_scalar(flat(ntop[:, :, :]), flat(top[:, :, :]), -1.0, None, ALU.mult).then_inc(masked, 1)

        def make_share(gi, n):
            head = gi * HPG + n
            dve.wait_ge(exps_done, head + 1)
            own.link(v.reciprocal(flat(total[n % 2][:, :, :]), flat(total[n % 2][:, :, :])))
            if not (isinstance(gi, int) and gi * HPG + n < 2):
                dve.wait_ge(probs_ready, head - 1)
            tt(share[n % 2][:, :, :], total[n % 2][:, :, :],
               gate[:, bass.ds(head, 1), :, :].rearrange("p a b t -> p (a b) t"), ALU.mult).then_inc(share_ready, 1)

        def take_head(gi, n):
            head = gi * HPG + n
            dve.wait_ge(o_done, head + 1)
            own.link(v.tensor_copy(o_hi[:, bass.ds(head, 1), :].rearrange("p a s -> p (a s)"), m[1][:, 0:S]))
            tt(o_lo[:, bass.ds(head, 1), :].rearrange("p a s -> p (a s)"), m[1][:, 0:S],
               o_hi[:, bass.ds(head, 1), :].rearrange("p a s -> p (a s)").bitcast(F32), ALU.subtract).then_inc(o_ready, 1)

        def attention(gi, slot):
            n = slot // 2
            if slot % 2 == 0:
                if real(gi, n - 3):
                    take_head(gi, n - 3)
            else:
                if real(gi, n - 1):
                    make_share(gi, n - 1)
                if real(gi, n) and n < HPG:
                    mask_scores(gi, n)

        def attentions(gi, slots=NB):
            return {s: lambda s=s: attention(gi, s) for s in range(slots)}

        q_scale = DH ** -0.5
        splits(Pos(C_Q), NB, {3: compressed})
        take(B_Q, q_t[:, :, :], MIX, q_scale)
        splits(Pos(C_Q + NB), NB, attentions(0))
        take(B_Q + 1, q_t[:, :, :], MIX, q_scale)
        with own.loop(1, GROUPS - 1, 4 * HPG) as gi:
            splits(Pos(C_Q + NB, gi, NB), NB, attentions(gi))
            take(B_Q + 1, q_t[:, :, :], MIX, q_scale)

        def out_block(number, n):
            kts = bass.ds(n * FT, FT)
            tt(h[:, kts, :], psum(number), h[:, kts, :], ALU.add).then_inc(taken, 1)
            dve.wait_ge(taken, n + (B_OUT + 1))
            for f in range(FT):
                operand(bass.ds(n * FT + f, 1), FFN, n * FT + (KT + f + 1))

        def first_out():
            dve.wait_ge(chunks_done, C_OUT + 14)
            out_block(B_OUT, 0)

        splits(Pos(C_OUT), 2 * NB, attentions(3, ATT_SLOTS + 1) | {14: first_out})
        out_block(B_OUT + 1, 1)
        with dve.Fori(2, 4) as n:
            splits(Pos(C_OUT, n, NB), NB)
            out_block(B_OUT + 1, n)

        def up(i, first):
            splits(Pos(C_UP, i, 2 * NB), NB, {4: lambda: variance(2)} if first else None)
            if first:
                dve.wait_ge(rms_ready, 2)
            take(B_UP, f_a[:, :, :], FFN)

            def gated():
                dve.wait_ge(up_sig, i + 1)
                own.link(tt(f_a[:, :, :], f_a[:, :, :], f_b[:, :, :], ALU.mult))

            splits(Pos(C_UP + NB, i, 2 * NB), NB, {1: gated})
            take(B_UP + 1, f_b[:, :, :], FFN)
            dve.wait_ge(taken, i * 2 + (B_UP + 2))
            tt(f_b[:, :, :], f_b[:, :, :], f_a[:, :, :], ALU.mult).then_inc(up_prod, 1)
            dve.wait_ge(fh_ready, i + 1)
            kts = bass.ds(i * FT, FT)
            tt(f_lo[:, kts, :], f_b[:, :, :], f_hi[:, kts, :].bitcast(F32), ALU.subtract).then_inc(f_ready, 1)

        up(0, True)
        with own.loop(1, NUP, 1) as i:
            up(i, False)

        def down(i, b):
            splits(Pos(C_DOWN + b * ND, i, 2 * ND), ND)
            kts = bass.ds(i * (2 * FT) + b * FT, FT)
            tt(h[:, kts, :], psum(B_DOWN + b), h[:, kts, :], ALU.add).then_inc(taken, 1)
            dve.wait_ge(taken, i * 2 + (B_DOWN + b + 1))
            dve.wait_ge(stats_ready, i * 4 + (8 + 2 * b))
            for f in range(FT):
                kt = bass.ds(i * (2 * FT) + (b * FT + f), 1)
                last = v.tensor_scalar(f_a[:, f, :], h[:, kt, :].rearrange("p a s -> p (a s)"),
                                       gains[:, FINAL, kt], None, ALU.mult)
            last.then_inc(hg_ready, 1)
            for f in range(FT):
                operand(bass.ds(i * (2 * FT) + (b * FT + f), 1), None, i * (2 * FT) + (2 * KT + b * FT + f + 1))

        with dve.Fori(0, 2) as i:
            down(i, 0)
            down(i, 1)

        def second_variance():
            dve.wait_ge(rms_ready, 3)
            own.link(tt(rtmp[:, :], rms[:, FINAL, :], rms[:, FINAL, :], ALU.mult))
            own.link(tt(rtmp[:, :], rtmp[:, :], m[1][:, 0:S + TT], ALU.mult))
            own.link(v.tensor_scalar(rtmp[:, :], rtmp[:, :], 1.0 / D, EPS, ALU.mult, ALU.add))
            v.reciprocal(rtmp[:, :], rtmp[:, :]).then_inc(var_ready, 1)

        def mlstm(i, first):
            at, number = ml_block(i, 0)
            the_set = ml_set(i, 0)
            splits(at, NB, {5: lambda: variance(4), 7: second_variance} if first else None)
            if first:
                dve.wait_ge(rms_ready, 4)
                own.link(tt(rms[:, PRE, :], rms[:, PRE, :], rms[:, FINAL, :], ALU.mult))
            for t in range(TT):
                v.tensor_scalar(t1[:, t, :], sets[the_set][:, t * PG:(t + 1) * PG], col(PRE, t), None, ALU.mult)
            tt(t1[:, 2:4, :], sets[the_set][:, BLK:].rearrange("p (f s) -> p f s", f=2), rows(PRE, 2),
               ALU.mult).then_inc(taken, 1)
            if first:
                splits(Pos(C_ML + NB), 1)
                dve.wait_ge(decay_in, 64)
                for t in range(TT):
                    last = stt(g_pre[:, t, :], sets[(B_ML + 1) % 2][:, t * BLK:t * BLK + 2 * MH], col(PRE, t),
                               g_bias[:, :], ALU.mult, ALU.add)
                last.then_inc(taken, 1)
                dve.wait_ge(taken, B_ML + 2)
                forget = g_pre[:, :, MH:2 * MH]
                stt(g_t[:, 0, :, :], forget, -1.0, forget, ALU.mult, ALU.min).then_inc(g2_pre, 1)
            dve.wait_ge(z_sig, i + 1)
            own.link(tt(t1[:, 2:4, :], t1[:, 2:4, :], t2[:, 0:2, :], ALU.mult))

            def take_pooled():
                dve.wait_ge(pool_done, i + 1)
                v.tensor_copy(flat(t2[:, 0:2, :]), m[0][:, :]).then_inc(pool_ready, 1)

            def take_mixed():
                dve.wait_ge(mix_done, i + 1)
                dve.wait_ge(cur_in, i * 16 + 16)
                for k in range(2):
                    last = stt(t2[:, 2 + k, :], m[1][:, k * S:(k + 1) * S], cur[:, P_SC + k:P_SC + k + 1],
                               t1[:, 2 + k, :], ALU.mult, ALU.mult)
                last.then_inc(yb_made, 1)

            def yb_low():
                dve.wait_ge(ybh_ready, i + 1)
                kts = bass.ds(i * 2, 2)
                tt(yb_lo[:, kts, :], t2[:, 2:4, :], yb_hi[:, kts, :].bitcast(F32), ALU.subtract).then_inc(yb_ready, 1)

            def convolve(b, params):
                tt(cq[:, :, 3:S + 3], sets[ml_set(i, b)][:, :].rearrange("p (f s) -> p f s", f=FT), rows(PRE),
                   ALU.mult).then_inc(taken, 1)
                dve.wait_ge(taken, ml_block(i, b)[1] + 1)
                for k in range(4):
                    for f in range(FT):
                        c = params + 5 * f
                        if k == 0:
                            last = v.tensor_scalar(t1[:, f, :], cq[:, f, 0:S], cur[:, c:c + 1], cur[:, c + 4:c + 5],
                                                   ALU.mult, ALU.add)
                        else:
                            last = stt(t1[:, f, :], cq[:, f, k:k + S], cur[:, c + k:c + k + 1], t1[:, f, :],
                                       ALU.mult, ALU.add)
                    if k < 3:
                        own.link(last)
                last.then_inc(conv_ready, 1)

            def silu(dst, b, scale):
                dve.wait_ge(conv_ready, i * 2 + (b + 1))
                dve.wait_ge(conv_sig, i * 2 + (b + 1))
                stt(dst, t1[:, :, :], scale, t2[:, :, :], ALU.mult, ALU.mult).then_inc(qkv_ready, 1)

            splits(ml_block(i, 1)[0], NB, {2: take_pooled, 4: take_mixed, 6: yb_low})
            convolve(1, Q_CONV)

            def cumulated():
                dve.wait_ge(f_done, 1)
                sums = m[3][:, 0:TT * MH].rearrange("p (t h) -> p t h", t=TT)
                v.tensor_copy(g_t[:, 1, :, :], sums)
                tt(g_t[:, 2, :, :], g_pre[:, :, 0:MH], sums, ALU.subtract).then_inc(g_ready, 1)

            def row_copy():
                dve.wait_ge(g_row_done, 1)
                v.tensor_copy(g_row, m[2][0:MH, 0:S]).then_inc(g_row_ready, 1)

            def log_forget():
                dve.wait_ge(g2_log, 1)
                stt(g_t[:, 0, :, :], g_pre[:, :, MH:2 * MH], 0.0, g_t[:, 1, :, :], ALU.min, ALU.subtract).then_inc(g2_f, 1)

            def arguments():
                dve.wait_ge(g_bc_done, 1)
                for k in range(MH):
                    src = m[k // 2][:, (k % 2) * S:(k % 2) * S + S]
                    for t in range(TT):
                        part = slice(t * P, (t + 1) * P + t * P)
                        last = v.tensor_tensor_reduce(out=decay[:, k, part], in0=src[:, 0:(t + 1) * P],
                                                      in1=causal[:, part], scale=1.0, scalar=0.0, op0=ALU.add,
                                                      op1=ALU.max, accum_out=g_max[:, k, t:t + 1])
                own.link(last)
                for t in range(TT):
                    last = stt(emm[:, t, :], g_max[:, :, t], -1.0, g_t[:, 1, t, :], ALU.mult, ALU.subtract)
                own.link(last)
                v.tensor_scalar(flat(g_max[:, :, :]), flat(g_max[:, :, :]), -1.0, None, ALU.mult).then_inc(decay_arg, 1)

            extras = {2: lambda: silu(qm[:, :, :], 0, MD ** -0.5)}
            if first:
                extras |= {0: log_forget, 1: cumulated, 3: row_copy, 4: arguments}
            splits(ml_block(i, 2)[0], NB, extras)
            convolve(2, K_CONV)
            splits(ml_block(i, 3)[0], NB, {2: lambda: silu(km[:, :, :], 1, 1.0)})
            if first:
                dve.wait_ge(decay_arg, 1)
            for t in range(TT):
                last = v.tensor_scalar(vm[:, t, :], sets[ml_set(i, 3)][:, t * BLK:(t + 1) * BLK], col(PRE, t), None, ALU.mult)
            last.then_inc(taken, 1)

            def head_probs(n):
                dve.wait_ge(ms_done, i * 2 + (n + 1))
                if n == 0:
                    dve.wait_ge(dec_ready, i + 1)
                if not (first and n == 0):
                    dve.wait_ge(mpt_done, i * 2 + n)
                for t in range(TT):
                    part = slice(t * P, (t + 1) * P + t * P)
                    last = v.tensor_tensor_reduce(out=pm[:, part], in0=m[0][:, part], in1=dec[:, n, part], scale=1.0, scalar=0.0,
                                                  op0=ALU.mult, op1=ALU.add, accum_out=den[:, 0, t:t + 1])
                own.link(last)
                own.link(stt(den[:, 1, :], den[:, 0, :], -1.0, den[:, 0, :], ALU.mult, ALU.max))
                own.link(tt(den[:, 1, :], den[:, 1, :], emm[:, :, bass.ds(i * 2 + n, 1)].rearrange("p t a -> p (t a)"), ALU.max))
                own.link(v.reciprocal(den[:, 1, :], den[:, 1, :]))
                for t in range(TT):
                    part = slice(t * P, (t + 1) * P + t * P)
                    last = v.tensor_scalar(pm[:, part], pm[:, part], den[:, 1, t:t + 1], None, ALU.mult)
                last.then_inc(mp_ready, 1)

            def head_out(n):
                dve.wait_ge(mh_done, i * 2 + (n + 1))
                v.tensor_copy(hn[:, 2 * n:2 * n + 2, :], m[2][:, :].rearrange("p (a s) -> p a s", a=2)).then_inc(mh_ready, 1)

            def head_var(n):
                dve.wait_ge(mn_done, i * 2 + (n + 1))
                if n == 0:
                    dve.wait_ge(o_sig, i + 1)
                own.link(v.tensor_scalar(t1[:, n, :], m[3][:, 0:S], 1.0 / MD, EPS, ALU.mult, ALU.add))
                v.reciprocal(t1[:, n, :], t1[:, n, :]).then_inc(mn_var, 1)

            def head_norm(n):
                dve.wait_ge(mn_root, i * 2 + (n + 1))
                dve.wait_ge(mh_ready, i * 2 + (n + 1))
                for f in range(2 * n, 2 * n + 2):
                    last = stt(hn[:, f, :], hn[:, f, :], cur[:, N_W + f:N_W + f + 1], t1[:, 2 + n, :], ALU.mult, ALU.mult)
                if n == 0:
                    own.link(last)
                else:
                    last.then_inc(cur_free, 1)

            def gate_out():
                dve.wait_ge(cur_free, i + 1)
                dve.wait_ge(o_sig, i + 1)
                own.link(tt(hn, hn, oz[:, :, :], ALU.mult))

            splits(ml_block(i, 4)[0], NB, {2: lambda: head_probs(0), 5: lambda: head_out(0), 6: lambda: head_probs(1)})
            tt(t1[:, :, :], sets[ml_set(i, 4)][:, :].rearrange("p (f s) -> p f s", f=FT), rows(PRE), ALU.mult).then_inc(taken, 1)
            splits(ml_block(i, 5)[0], NB, {1: lambda: head_out(1), 2: lambda: head_var(0), 4: lambda: head_var(1),
                                           5: lambda: head_norm(0), 6: lambda: head_norm(1), 7: gate_out})
            tt(t1[:, :, :], sets[ml_set(i, 5)][:, :].rearrange("p (f s) -> p f s", f=FT), rows(PRE), ALU.mult).then_inc(taken, 1)
            dve.wait_ge(taken, ml_block(i, 5)[1] + 1)
            own.link(tt(hn, hn, t1[:, :, :], ALU.mult))
            dve.wait_ge(zg_sig, i + 1)
            tt(hn, hn, t2[:, :, :], ALU.mult).then_inc(ya_made, 1)
            dve.wait_ge(yah_ready, i + 1)
            kts = bass.ds(i * FT, FT)
            tt(ya_lo[:, kts, :], hn, ya_hi[:, kts, :].bitcast(F32), ALU.subtract).then_inc(ya_ready, 1)

        v.memset(cq[:, :, 0:3], 0.0)
        mlstm(0, True)
        with own.loop(1, 4, ML_LINKS) as i:
            mlstm(i, False)

        with dve.Fori(0, 4) as i:
            splits(Pos(C_MG, i, NMG), NB)
            take(B_MG, m_a[:, :, :], PRE)
            splits(Pos(C_MG + NB, i, NMG), NB)
            take(B_MG + 1, m_b[:, :, :], PRE)
            splits(Pos(C_MG + 2 * NB, i, NMG), NB)
            dve.wait_ge(ga_sig, i + 1)
            tt(m_a[:, :, :], psum(B_MG + 2), m_a[:, :, :], ALU.mult).then_inc(taken, 1)
            splits(Pos(C_MG + 3 * NB, i, NMG), NB // 2)
            dve.wait_ge(gb_sig, i + 1)
            tt(m_b[:, :, :], psum(B_MG + 3), m_b[:, :, :], ALU.mult).then_inc(taken, 1)
            dve.wait_ge(taken, i * 4 + (B_MG + 4))
            tt(m_t[:, :, :], m_a[:, :, :], m_b[:, :, :], ALU.add).then_inc(mg_made, 1)
            dve.wait_ge(mh2_ready, i + 1)
            kts = bass.ds(i * FT, FT)
            tt(m_lo[:, kts, :], m_t[:, :, :], m_hi[:, kts, :].bitcast(F32), ALU.subtract).then_inc(m_ready, 1)

        def out_taken(n):
            v.tensor_copy(out_t[:, n * FT:(n + 1) * FT, :], psum(B_WO + n)).then_inc(taken, 1)
            for kt in range(n * FT, (n + 1) * FT):
                stt(h[:, kt, :], h[:, kt, :], gains[:, FINAL, kt:kt + 1], row(FINAL), ALU.mult, ALU.mult)

        for n in range(4):
            splits(Pos(C_WO + n * NB), NB)
            out_taken(n)
        variance(5)
        dve.wait_ge(rms_ready, 5)
        for n in range(4):
            for f in range(FT):
                kt = n * FT + f
                last = stt(y_t[:, kt, :], out_t[:, kt, :], gains[:, POST, kt:kt + 1], row(POST), ALU.mult, ALU.mult)
            own.link(last)
            kts = slice(n * FT, (n + 1) * FT)
            tt(y_t[:, kts, :], y_t[:, kts, :], h[:, kts, :], ALU.add).then_inc(y_ready, 1)

    @block.tensor
    def _(pe):
        mm = nc.tensor.matmul

        def await_set(number, same=False):
            if isinstance(number, int):
                if number - 1 + same > 0:
                    pe.wait_ge(taken, number - 1 + same)
            else:
                pe.wait_ge(taken, number + (same - 1))

        def features(at, j, out, hi, lo, kts, first, ft=FT, ft0=0, last_in_bank=None):
            slot = at.slot(j)
            for k, kt in enumerate(kts):
                for f in range(ft):
                    c = k * BLK + (ft0 + f) * P
                    o = out[:, (ft0 + f) * S:(ft0 + f + 1) * S]
                    starts = first and k == 0 and f % 2 == 0
                    mm(o, w_hi[slot][:, c:c + P], hi[:, kt, :], start=starts, stop=False, skip_group_check=True)
                    mm(o, w_hi[slot][:, c:c + P], lo[:, kt, :], start=False, stop=False, skip_group_check=True)
                    last = mm(o, w_lo[slot][:, c:c + P], hi[:, kt, :], start=False, stop=True, skip_group_check=True)
            return last

        def tokens(at, j, out, hi, lo, kts, first, width, cols=0, per_k=BLK, pitch=BLK):
            slot = at.slot(j)
            for k, kt in enumerate(kts):
                for t in range(TT):
                    o = out[:, t * pitch:t * pitch + width]
                    c = k * per_k + cols
                    x = slice(t * P, (t + 1) * P)
                    starts = first and k == 0 and (t == 0 or pitch == BLK)
                    mm(o, hi[:, kt, x], w_hi[slot][:, c:c + width], start=starts, stop=False, skip_group_check=True)
                    mm(o, hi[:, kt, x], w_lo[slot][:, c:c + width], start=False, stop=False, skip_group_check=True)
                    last = mm(o, lo[:, kt, x], w_hi[slot][:, c:c + width], start=False, stop=True, skip_group_check=True)
            return last

        def chunk(at, j, wait, emit):
            pe.wait_ge(lo_ready, at.at(j) + 1)
            if wait:
                pe.wait_ge(*wait)
            emit().then_inc(chunks_done, 1)

        def gemm(at, number, the_set, n=NB, ready=None, hi=x_hi, lo=x_lo, same=False, tokenwise=False, steps=None):
            await_set(number, same)
            out = sets[the_set]
            for j in range(n):
                kts = (2 * j, 2 * j + 1)
                wait = ready(kts[1]) if ready else None
                if tokenwise:
                    chunk(at, j, wait, lambda: tokens(at, j, out, hi, lo, kts, j == 0, BLK))
                else:
                    chunk(at, j, wait, lambda: features(at, j, out, hi, lo, kts, j == 0))
                if steps and j in steps:
                    steps[j]()

        def operand_ready(count):
            return lambda kt: (x_ready, count + kt + 1)

        pe.wait_ge(consts, 2)
        pe.wait_ge(small_in, 96)
        for t in range(TT):
            for c in range(NC):
                o = (t * NC + c) * HEADS
                mm(m[2][:, o:o + HEADS], onehot[:, c, t * P:(t + 1) * P], rel[:, :], start=True, stop=True)
        mm(m[3][0:HEADS, :], rel[:, :], ohd[:, :], start=True, stop=True).then_inc(rel_done, 1)

        def stats(k, bank, count, signal=True):
            pe.wait_ge(stats_ready, count)
            mm(m[bank][:, 0:S], ones[:, :], stat[:, k, :], start=True, stop=True)
            for t in range(TT):
                last = mm(m[bank][:, S + t:S + t + 1], stat[:, k, t * P:(t + 1) * P], ones[:, 0:1], start=True, stop=True)
            if signal:
                last.then_inc(stats_sum, 1)

        def flip_bias(half):
            pe.wait_ge(consts, 3)
            pe.wait_ge(bias_in, 16)
            pe.wait_ge(bias_c_ready, 1)
            if half:
                pe.wait_ge(bias_ready, 1)
            for n in range(4):
                head = half * 8 + 2 * n
                last = mm(m[n][:, :], flip[:, :], bias[:, head:head + 2, :].rearrange("p a s -> p (a s)"),
                          start=True, stop=True)
            last.then_inc(flip_done, 1)

        steps = {0: {4: lambda: stats(0, 0, 4)}, 1: {1: lambda: flip_bias(0), 4: lambda: flip_bias(1)}}
        for n in range(4):
            gemm(Pos(C_KV + n * NB), B_KV + n, n % 2, ready=operand_ready(0) if n == 0 else None, steps=steps.get(n))
        for n in range(4, 6):
            gemm(Pos(C_KV + n * NB), B_KV + n, n % 2, tokenwise=True)
        await_set(B_G1)
        chunk(Pos(C_G1), 0, None, lambda: tokens(Pos(C_G1), 0, sets[B_G1 % 2], x_hi, x_lo, range(KT), True, 48, per_k=48))

        for n in range(2):
            await_set(B_CMP + n)
            out = sets[(B_CMP + n) % 2]
            at = Pos(C_CMP + n * NB)
            pe.wait_ge(blk_ready, n + 1)
            for j in range(NB):
                pe.wait_ge(lo_ready, at.at(j) + 1)
                s = at.slot(j)
                for k in range(4):
                    kt = 4 * j + k
                    for f in range(2):
                        c = k * CH + f * P
                        o = out[:, f * BLK:f * BLK + GROUPS * NC]
                        mm(o, w_hi[s][:, c:c + P], blk_hi[:, n, kt, :], start=kt == 0, stop=False, skip_group_check=True)
                        mm(o, w_hi[s][:, c:c + P], blk_lo[:, n, kt, :], start=False, stop=False, skip_group_check=True)
                        last = mm(o, w_lo[s][:, c:c + P], blk_hi[:, n, kt, :], start=False, stop=True, skip_group_check=True)
                last.then_inc(chunks_done, 1)

        def compressed():
            pe.wait_ge(hid_ready, 2)
            for f in range(2):
                mm(m[0][:, 0:GROUPS * NC], w2[:, 0, f, :], hid[:, 0, f, :], start=f == 0, stop=f == 1)
            for gr in range(GROUPS):
                for f in range(2):
                    last = mm(m[1][0:NC, gr * DH:(gr + 1) * DH], hid[:, 1, f, gr * NC:(gr + 1) * NC], w2[:, 1, f, :],
                              start=f == 0, stop=f == 1)
            last.then_inc(kvc_sum, 1)

        def scores(gi, n):
            if n == 0:
                pe.wait_ge(taken, gi + (B_Q + 1))
                pe.wait_ge(kg_ready, gi + 1)
            if real(gi, n - 1):
                pe.wait_ge(masked, gi * HPG + n)
            if real(gi, n - 3):
                pe.wait_ge(o_ready, gi * HPG + (n - 2))
            q0, q1 = q_t[:, n, 0:P], q_t[:, n, P:S]
            mm(m[0][:, 0:P], q0, k_g[:, 0, 0:P], start=True, stop=True)
            mm(m[0][:, P:TRI], q1, k_g[:, 0, :], start=True, stop=True)
            mm(m[0][:, TRI:TRI + NC], q0, k_cg[:, :], start=True, stop=True)
            mm(m[0][:, TRI + 16:TRI + 16 + NC], q1, k_cg[:, :], start=True, stop=True)
            mm(m[1][:, 0:P], q0, k_g[:, 1, 0:P], start=True, stop=True)
            mm(m[1][:, P:TRI], q1, k_g[:, 1, :], start=True, stop=True).then_inc(scores_done, 1)

        def transposes(gi, n):
            pe.wait_ge(probs_ready, gi * HPG + (n + 1))
            if real(gi, n - 1):
                pe.wait_ge(pt_ready, gi * HPG + n)
            pr = prob[n % 2]
            tr = nc.tensor.transpose
            for b, o in ((2, O_SEL), (3, O_WIN)):
                for k in range(3):
                    tr(m[b][:, k * P:(k + 1) * P], pr[:, o + k * P:o + (k + 1) * P], ident[:, :])
            tr(m[2][0:NC, TRI:BLK], pr[:, O_CMP:O_CMP + NC], ident[:, :])
            tr(m[3][0:NC, TRI:BLK], pr[:, O_CMP + 16:O_CMP + 16 + NC], ident[:, :]).then_inc(pt_done, 1)

        def values(gi, n):
            if n == 0:
                pe.wait_ge(vg_ready, gi + 1)
            pe.wait_ge(pt_ready, gi * HPG + (n + 1))
            if n + 2 < HPG:
                pe.wait_ge(masked, gi * HPG + (n + 3))
            if real(gi, n - 1):
                pe.wait_ge(o_ready, gi * HPG + n)
            for b in range(2):
                mm(m[1][:, 0:S], v_g[:, b, 0, :], prob_t[:, b, 0:S], start=b == 0, stop=False)
                mm(m[1][:, P:S], v_g[:, b, 1, :], prob_t[:, b, S:TRI], start=False, stop=False)
            mm(m[1][:, 0:S], v_cg[:, :], prob_ct[:, :], start=False, stop=True).then_inc(o_done, 1)

        def attention(gi, slot):
            n = slot // 2
            if slot % 2 == 0:
                if n < HPG:
                    scores(gi, n)
            else:
                if real(gi, n - 2):
                    values(gi, n - 2)
                if real(gi, n - 1):
                    transposes(gi, n - 1)

        def attentions(gi, slots=NB):
            return {s: lambda s=s: attention(gi, s) for s in range(slots)}

        gemm(Pos(C_Q), B_Q, B_Q % 2, steps={2: compressed})
        gemm(Pos(C_Q + NB), B_Q + 1, (B_Q + 1) % 2, steps=attentions(0))
        with pe.Fori(1, GROUPS - 1) as gi:
            gemm(Pos(C_Q + NB, gi, NB), gi + (B_Q + 1), (B_Q + 1) % 2, same=True, steps=attentions(gi))

        def heads_ready(kt):
            return (o_ready, kt + 1)

        await_set(B_OUT)
        at, slot = Pos(C_OUT), 0
        for block_no, j0, count in ((0, 0, 6), (1, 0, 6), (0, 6, 2), (1, 6, 2)):
            for j in range(j0, j0 + count):
                kts = (2 * j, 2 * j + 1)
                if (block_no, j) == (1, 0):
                    await_set(B_OUT + 1)
                chunk(at, slot, heads_ready(kts[1]),
                      lambda: features(at, slot, sets[(B_OUT + block_no) % 2], o_hi, o_lo, kts, j == 0))
                if slot < ATT_SLOTS:
                    attention(3, slot)
                slot += 1
        with pe.Fori(2, 4) as n:
            gemm(Pos(C_OUT, n, NB), n + B_OUT, (B_OUT + 1) % 2, same=True, hi=o_hi, lo=o_lo)

        def up(i, first):
            gemm(Pos(C_UP, i, 2 * NB), i * 2 + B_UP, B_UP % 2, ready=operand_ready(KT) if first else None,
                 steps={3: lambda: stats(0, 0, 8)} if first else None)
            gemm(Pos(C_UP + NB, i, 2 * NB), i * 2 + (B_UP + 1), (B_UP + 1) % 2)

        up(0, True)
        with pe.Fori(1, NUP) as i:
            up(i, False)
        with pe.Fori(0, 2) as i:
            for b in range(2):
                gemm(Pos(C_DOWN + b * ND, i, 2 * ND), i * 2 + (B_DOWN + b), (B_DOWN + b) % 2, n=ND,
                     hi=f_hi, lo=f_lo, ready=(lambda kt: (f_ready, kt // FT + 1)) if b == 0 else None)

        def mlstm(i, first):
            at, number = ml_block(i, 0)
            out = sets[ml_set(i, 0)]
            await_set(number)
            for j in range(NB):
                kts = (2 * j, 2 * j + 1)

                def pool_chunk():
                    tokens(at, j, out, x_hi, x_lo, kts, j == 0, PG, pitch=PG)
                    return features(at, j, out, x_hi, x_lo, kts, j == 0, ft=2, ft0=2)

                chunk(at, j, (x_ready, 2 * KT + kts[1] + 1) if first else None, pool_chunk)
                if first and j == 4:
                    stats(0, 0, 16)
                    stats(1, 1, 16)
            if first:
                await_set(B_ML + 1)
                gates_at = Pos(C_ML + NB)
                chunk(gates_at, 0, None, lambda: tokens(gates_at, 0, sets[(B_ML + 1) % 2], x_hi, x_lo, range(KT), True,
                                                        2 * MH, per_k=2 * MH))

            def pooled():
                pe.wait_ge(taken, number + 1)
                pe.wait_ge(cur_in, i * 16 + 16)
                if not first:
                    pe.wait_ge(mp_ready, i * 2)
                for c in range(2):
                    for s in range(TT):
                        last = mm(m[0][:, c * S:(c + 1) * S], t1[:, s, c * P:(c + 1) * P],
                                  cur[:, P_BAND + s * S:P_BAND + (s + 1) * S], start=s == 0, stop=s == 1)
                last.then_inc(pool_done, 1)

            def mixed():
                pe.wait_ge(pool_ready, i + 1)
                if not first:
                    pe.wait_ge(mpt_ready, i * 2)
                for o in range(2):
                    for c in range(2):
                        w = P_W + c * PG + o * P
                        last = mm(m[1][:, o * S:(o + 1) * S], cur[:, w:w + P], t2[:, c, :], start=c == 0, stop=c == 1)
                last.then_inc(mix_done, 1)

            def forget_sums():
                pe.wait_ge(g2_f, 1)
                mm(m[3][:, 0:MH], tri, g_t[:, 0, 0, :], start=True, stop=True)
                mm(m[3][:, MH:2 * MH], ones[:, :], g_t[:, 0, 0, :], start=True, stop=False)
                mm(m[3][:, MH:2 * MH], tri, g_t[:, 0, 1, :], start=False, stop=True).then_inc(f_done, 1)

            def g_rows():
                pe.wait_ge(g_ready, 1)
                for t in range(TT):
                    last = nc.tensor.transpose(m[2][0:MH, t * P:(t + 1) * P], g_t[:, 2, t, :], ident[:, :])
                last.then_inc(g_row_done, 1)

            def g_broadcast():
                pe.wait_ge(g_row_ready, 1)
                pe.wait_ge(yb_made, 1)
                for k in range(MH):
                    last = mm(m[k // 2][:, (k % 2) * S:(k % 2 + 1) * S], sel[:, k * P:(k + 1) * P], g_row,
                              start=True, stop=True)
                last.then_inc(g_bc_done, 1)

            gemm(ml_block(i, 1)[0], ml_block(i, 1)[1], ml_set(i, 1), steps={1: pooled, 3: mixed})
            gemm(ml_block(i, 2)[0], ml_block(i, 2)[1], ml_set(i, 2),
                 steps={0: forget_sums, 2: g_rows, 3: g_broadcast} if first else None)
            gemm(ml_block(i, 3)[0], ml_block(i, 3)[1], ml_set(i, 3), tokenwise=True)

            def head_scores(n):
                pe.wait_ge(qkv_ready, i * 2 + 2)
                if first and n == 0:
                    pe.wait_ge(decay_ready, 2)
                if not (first and n == 0):
                    pe.wait_ge(mp_ready, i * 2 + n)
                if n == 0:
                    pe.wait_ge(yb_made, i + 1)
                for t in range(TT):
                    for k in range(2):
                        last = mm(m[0][:, t * P:(t + 1) * P + t * P], qm[:, 2 * n + k, t * P:(t + 1) * P],
                                  km[:, 2 * n + k, 0:(t + 1) * P], start=k == 0, stop=k == 1)
                last.then_inc(ms_done, 1)

            def head_transposes(n):
                pe.wait_ge(mp_ready, i * 2 + (n + 1))
                if not (first and n == 0):
                    pe.wait_ge(mpt_ready, i * 2 + n)
                for k in range(3):
                    last = nc.tensor.transpose(m[1][:, k * P:(k + 1) * P], pm[:, k * P:(k + 1) * P], ident[:, :])
                last.then_inc(mpt_done, 1)

            def head_values(n):
                pe.wait_ge(mpt_ready, i * 2 + (n + 1))
                if n == 0:
                    pe.wait_ge(taken, ml_block(i, 3)[1] + 1)
                if not (first and n == 0):
                    pe.wait_ge(mh_ready, i * 2 + n)
                for f in range(2):
                    c = n * MD + f * P
                    mm(m[2][:, f * S:(f + 1) * S], vm[:, 0, c:c + P], pm_t[:, 0:S], start=True, stop=False)
                    last = mm(m[2][:, f * S + P:(f + 1) * S], vm[:, 1, c:c + P], pm_t[:, S:TRI], start=False, stop=True)
                last.then_inc(mh_done, 1)

            def head_squares(n):
                pe.wait_ge(mh_sq, i * 2 + (n + 1))
                if not (first and n == 0):
                    pe.wait_ge(mn_var, i * 2 + n)
                for f in range(2):
                    last = mm(m[3][:, 0:S], ones[:, :], t2[:, 2 * n + f, :], start=f == 0, stop=f == 1)
                last.then_inc(mn_done, 1)

            gemm(ml_block(i, 4)[0], ml_block(i, 4)[1], ml_set(i, 4),
                 steps={1: lambda: head_scores(0), 3: lambda: head_transposes(0), 4: lambda: head_values(0),
                        5: lambda: head_scores(1), 7: lambda: head_transposes(1)})
            gemm(ml_block(i, 5)[0], ml_block(i, 5)[1], ml_set(i, 5),
                 steps={0: lambda: head_values(1), 1: lambda: head_squares(0), 3: lambda: head_squares(1)})

        mlstm(0, True)
        with pe.Fori(1, 4) as i:
            mlstm(i, False)

        with pe.Fori(0, 4) as i:
            gemm(Pos(C_MG, i, NMG), i * 4 + B_MG, B_MG % 2)
            gemm(Pos(C_MG + NB, i, NMG), i * 4 + (B_MG + 1), (B_MG + 1) % 2)
            gemm(Pos(C_MG + 2 * NB, i, NMG), i * 4 + (B_MG + 2), B_MG % 2, hi=ya_hi, lo=ya_lo,
                 ready=lambda kt: (ya_ready, kt // FT + 1))
            gemm(Pos(C_MG + 3 * NB, i, NMG), i * 4 + (B_MG + 3), (B_MG + 1) % 2, n=NB // 2, hi=yb_hi, lo=yb_lo,
                 ready=lambda kt: (yb_ready, kt // 2 + 1))
        with pe.Fori(0, 2) as i:
            for b in range(2):
                gemm(Pos(C_WO + b * NB, i, 2 * NB), i * 2 + (B_WO + b), (B_WO + b) % 2, hi=m_hi, lo=m_lo,
                     ready=(lambda kt: (m_ready, kt // FT + 1)) if b == 0 else None)
        stats(0, 0, 20)

    ctx.close()


def bucket(n):
    exact = BUCKETS // 2
    if n < exact:
        return n
    large = np.log(np.float32(n) / np.float32(exact)) / np.float32(math.log(MAX_DIST / exact))
    return min(exact + int(np.float32(large) * np.float32(BUCKETS - exact)), BUCKETS - 1)


def shape_constants():
    onehot = np.zeros((BUCKETS + 1, NC, S), np.float32)
    for c in range(NC):
        for t in range(S):
            dist = t - (CS * c + CB - 1)
            if dist >= 0:
                onehot[bucket(dist), c, t] = 1
            else:
                onehot[BUCKETS, c, t] = NEG
    ohd = np.zeros((BUCKETS + 1, 2 * S), np.float32)
    for i in range(2 * S):
        if i < S:
            ohd[bucket(S - 1 - i), i] = 1
        else:
            ohd[BUCKETS, i] = NEG
    t = np.arange(S).reshape(TT, P).T
    valid = (t >= CB - 1).astype(np.float32)
    p = np.arange(P)
    causal = np.zeros((P, TRI), np.float32)
    causal[:, 0:P] = np.where(p[None, :] <= p[:, None], 0, NEG)
    causal[:, P:] = np.where(np.arange(S)[None, :] <= p[:, None] + P, 0, NEG)
    tri = (p[:, None] <= p[None, :]).astype(np.float32)
    sel = np.zeros((MH, MH, P), np.float32)
    for k in range(MH):
        sel[k, k] = 1
    band = np.zeros((len(POOLS), S, S), np.float32)
    for n, w in enumerate(POOLS):
        for t_ in range(S):
            lo = max(t_ + 1 - w, 0)
            band[n, lo:t_ + 1, t_] = np.float32(1) / np.float32(t_ + 1 - lo)
            band[n, t_, t_] -= 1
    return {"onehot": onehot, "ohd": ohd, "valid": valid, "causal": causal, "tri": tri,
            "sel": sel.reshape(MH, MH * P)}, band


def blocks(w):
    k, n = w.shape
    return w.reshape(k // (2 * P), 2, P, n // BLK, BLK).transpose(3, 0, 2, 1, 4).reshape(n // BLK, k // (2 * P), P, CC)


def lay_out(a):
    def vec(x):
        return x.reshape(-1, P).T

    w_in = a["nsa_w_in"][0]
    kvw = HEADS * DH
    k_width = GROUPS * DH
    part = [w_in[:, kvw + n * k_width:kvw + (n + 1) * k_width] for n in range(6)]
    stream = [blocks(part[n])[0] for n in (0, 1, 2, 4, 3, 5)]

    def gate_chunk(w):
        out = np.zeros((1, P, CC), np.float32)
        out[0, :, :KT * w.shape[1]] = w.reshape(KT, P, w.shape[1]).transpose(1, 0, 2).reshape(P, -1)
        return out

    stream.append(gate_chunk(w_in[:, kvw + 6 * k_width:]))
    for name in ("cmp_w1_k", "cmp_w1_v"):
        stream.append(a[name][0].reshape(NB, 4, P, CH).transpose(0, 2, 1, 3).reshape(NB, P, CC))
    stream += list(blocks(w_in[:, :kvw]))
    o = blocks(a["nsa_w_out"][0])
    stream += [o[0][:6], o[1][:6], o[0][6:], o[1][6:], o[2], o[3]]
    up = a["ffn_w_in"][0]
    gate_part, value_part = blocks(up[:, :FF]), blocks(up[:, FF:])
    for j in range(NUP):
        stream += [gate_part[j], value_part[j]]
    stream += list(blocks(a["ffn_w_out"][0]))

    w2 = a["w_in_2"][0]
    at = 0
    cols = {}
    for name, width in (("q", D), ("k", D), ("v", D), ("o", D), ("z", D), ("gates", 2 * MH), ("u", len(POOLS) * PG),
                        ("zb", len(POOLS) * PG), ("ga", D), ("gb", D)):
        cols[name] = w2[:, at:at + width]
        at += width
    big = {n: blocks(cols[n]) for n in ("q", "k", "v", "o", "z", "ga", "gb")}
    for i in range(4):
        uz = np.concatenate([cols["u"][:, i * PG:(i + 1) * PG], cols["zb"][:, i * PG:(i + 1) * PG]], axis=1)
        stream.append(blocks(uz)[0])
        if i == 0:
            stream.append(gate_chunk(cols["gates"]))
        stream += [big[n][i] for n in ("q", "k", "v", "o", "z")]
    pa, pb = blocks(a["w_proj_mlstm_2"][0]), blocks(a["w_proj_pool_2"][0])
    for i in range(4):
        stream += [big["ga"][i], big["gb"][i], pa[i], pb[i]]
    stream += list(blocks(a["w_out_2"][0]))

    constants, band = shape_constants()
    conv_w, conv_b = a["qk_conv_w_2"][0], a["qk_conv_b_2"][0]
    conv = np.concatenate([conv_w, conv_b[None]], axis=0).reshape(5, 2, 4, FT, P)
    cur = np.concatenate([
        conv.transpose(2, 4, 1, 3, 0).reshape(4, P, 2 * FT * 5),
        a["mlstm_norm_w_2"][0].reshape(4, FT, P).transpose(0, 2, 1),
        a["pool_scale_2"][0].reshape(4, 2, P).transpose(0, 2, 1),
        a["pool_w_2"][0].reshape(4, 2, P, PG).transpose(0, 2, 1, 3).reshape(4, P, 2 * PG),
        band.reshape(4, TT, P, S).transpose(0, 2, 1, 3).reshape(4, P, TT * S),
    ], axis=2)
    return {
        "x": a["x"][0].T.reshape(KT, P, S),
        "weights": np.concatenate(stream, axis=0),
        "gains": np.stack([vec(a["mix_norm_g"][0]), vec(a["ffn_norm_g"][0]), vec(a["final_norm_g"]),
                           vec(a["norm_pre_w_2"][0]), vec(a["norm_post_w_2"][0])], axis=1),
        "rel": a["rel_bias"],
        "w2": np.stack([a["cmp_w2_k"][0].reshape(2, P, DH), a["cmp_w2_v"][0].reshape(2, P, DH)]).transpose(2, 0, 1, 3),
        "pos": np.stack([a["cmp_pos_k"][0].T, a["cmp_pos_v"][0].T], axis=1),
        "g_bias": np.broadcast_to(np.concatenate([a["mlstm_i_bias_2"][0], a["mlstm_f_bias_2"][0]]), (P, 2 * MH)),
        "cur": cur,
        **constants,
    }


def kernel(**inputs):
    import concourse.bacc as bacc
    from concourse.bass_utils import run_bass_kernel_spmd

    nc = bacc.Bacc("TRN2", target_bir_lowering=False, num_devices=1)
    arrays = {f"in_{k}": np.ascontiguousarray(v) for k, v in lay_out({k: np.asarray(v) for k, v in inputs.items()}).items()}
    d = {k[3:]: nc.dram_tensor(k, v.shape, mybir.dt.from_np(v.dtype), kind="ExternalInput").ap() for k, v in arrays.items()}
    d["out"] = nc.dram_tensor("out", (KT, P, S), F32, kind="ExternalOutput").ap()
    program(nc, d)
    r = run_bass_kernel_spmd(nc, [arrays], core_ids=[0])
    return r.results[0]["out"].reshape(D, S).T.reshape(1, S, D)
```

```python
import math
from contextlib import ExitStack, contextmanager

import numpy as np

import concourse.bass as bass
from concourse import mybir

F32 = mybir.dt.float32
F32R = mybir.dt.float32r
ACT = mybir.ActivationFunctionType
ALU = mybir.AluOpType

P = 128
S = 256
D = 2048
TT = S // P
KT = D // P
HEADS, GROUPS, DH = 16, 4, 128
HPG = HEADS // GROUPS
CB, CS = 32, 16
NC = (S - CB) // CS + 1
BUCKETS, MAX_DIST = 32, 128
FF = 5632
FKT = FF // P
CH = 2 * DH
MH, MD = 8, 256
POOLS = (2, 4, 8, 16)
PG = 256
EPS = 1e-6
NEG = -1e30

BLK, FT = 512, 4
CC = 1024
NB = KT // 2
ND = FKT // 2
RING = 4
AHEAD = 3
NUP = FF // BLK
NML = 6 * NB
NMG = 3 * NB + NB // 2
C_KV = 0
C_G1 = C_KV + 6 * NB
C_CMP = C_G1 + 1
C_Q = C_CMP + 2 * NB
C_OUT = C_Q + 4 * NB
C_UP = C_OUT + 4 * NB
C_DOWN = C_UP + 2 * NUP * NB
C_ML = C_DOWN + 4 * ND
C_MG = C_ML + 1 + 4 * NML
C_WO = C_MG + 4 * NMG
CHUNKS = C_WO + 4 * NB
B_KV, B_G1, B_CMP, B_Q, B_OUT, B_UP = 0, 6, 7, 9, 13, 17
B_DOWN = B_UP + 2 * NUP
B_ML = B_DOWN + 4
B_MG = B_ML + 1 + 4 * 6
B_WO = B_MG + 4 * 4

TRI = P + S
O_SEL, O_CMP, O_WIN = 0, TRI, TRI + 32
PCOLS = O_WIN + TRI

Q_CONV, K_CONV, N_W, P_SC, P_W = 0, 20, 40, 44, 46
P_BAND = P_W + TT * PG
CUR = P_BAND + TT * S

MIX, FFN, FINAL, PRE, POST = range(5)


WARM_UP = 27
ATT_SLOTS = 12
ML_LINKS = 20


def real(gi, n):
    return n < HPG and (not isinstance(gi, int) or gi * HPG + n >= 0)


class Pos:

    def __init__(self, base, i=0, n=0):
        if isinstance(i, int):
            base, i, n = base + i * n, 0, 0
        assert n % RING == 0
        self.base, self.i, self.n = base, i, n

    def at(self, j):
        return self.base + j if self.n == 0 else self.i * self.n + (self.base + j)

    def slot(self, j):
        return (self.base + j) % RING

    def lap(self, j):
        lap = (self.base + j) // RING
        return lap if self.n == 0 else self.i * (self.n // RING) + lap

    def exists(self, j):
        return self.n != 0 or self.base + j < CHUNKS

    def after_first_lap(self, j):
        return self.n != 0 or self.base + j >= RING


class Chain:

    def __init__(self, engine, done):
        self.engine, self.done, self.start, self.k, self.i, self.per = engine, done, 0, 0, 0, 0

    def link(self, instruction):
        self.k += 1
        instruction.then_inc(self.done, 1)
        base = self.start + self.k
        self.engine.wait_ge(self.done, base if isinstance(self.i, int) else self.i * self.per + base)

    @contextmanager
    def loop(self, start, end, per):
        self.start, self.k = self.start + self.k, 0
        with self.engine.Fori(start, end) as i:
            self.i, self.per = i, per
            self.start -= start * per
            yield i
            assert self.k == per, (self.k, per)
        self.start, self.k, self.i, self.per = self.start + end * per, 0, 0, 0


def program(nc, d):
    ctx = ExitStack()

    def sb(name, shape, dt=F32, scope=ctx):
        return scope.enter_context(nc.sbuf_tensor(name, shape, dt))

    def sem(name):
        return ctx.enter_context(nc.semaphore(name))

    raw = [sb(f"raw{n}", [P, CC]) for n in range(RING)]
    w_hi = [sb(f"w_hi{n}", [P, CC], F32R) for n in range(RING)]
    w_lo = [sb(f"w_lo{n}", [P, CC], F32R) for n in range(RING)]
    x_hi = sb("x_hi", [P, KT, S], F32R)
    x_lo = sb("x_lo", [P, KT, S], F32R)
    h = sb("h", [P, KT, S])
    ident = sb("ident", [P, P])
    ones = sb("ones", [P, P])
    gains = sb("gains", [P, 5, KT])
    gain2 = sb("gain2", [P, KT])
    stat = sb("stat", [P, 2, S])
    sq = sb("sq", [P, FT, S])
    rms = sb("rms", [P, 5, S + TT])
    rtmp = sb("rtmp", [P, S + TT])

    with ExitStack() as s1:
        k_sw = sb("k_sw", [P, 2, GROUPS, S], scope=s1)
        v_sw = sb("v_sw", [P, 2, TT, GROUPS * DH], scope=s1)
        bias = sb("bias", [P, HEADS, S + TT * NC], scope=s1)
        gate = sb("gate", [P, HEADS, 3, TT], scope=s1)
        g_sig = sb("g_sig", [3 * HEADS, S], scope=s1)
        q_t = sb("q_t", [P, HPG, S], scope=s1)
        v_g = sb("v_g", [P, 2, TT, DH], scope=s1)
        k_c = sb("k_c", [P, GROUPS, NC], scope=s1)
        v_c = sb("v_c", [NC, GROUPS, DH], scope=s1)
        v_cg = sb("v_cg", [NC, DH], scope=s1)
        w2 = sb("w2", [P, 2, 2, DH], scope=s1)
        pos = sb("pos", [P, 2, CB], scope=s1)
        valid = sb("valid", [P, TT], scope=s1)
        rel = sb("rel", [BUCKETS + 1, HEADS], scope=s1)
        hid_in = sb("hid_in", [GROUPS * NC, 2, CH], scope=s1)
        hid = sb("hid", [P, 2, 2, GROUPS * NC], scope=s1)
        with ExitStack() as s1a:
            ohd = sb("ohd", [BUCKETS + 1, 2 * S], scope=s1a)
            u_row = sb("u_row", [HEADS, 2 * S], scope=s1a)
        with ExitStack() as s1b:
            kv_c = sb("kv_c", [P, 2, GROUPS, S], scope=s1b)
            blk_in = sb("blk_in", [P, CB, GROUPS, NC], scope=s1b)
            blk_hi = sb("blk_hi", [P, 2, CB, GROUPS * NC], F32R, scope=s1b)
            blk_lo = sb("blk_lo", [P, 2, CB, GROUPS * NC], F32R, scope=s1b)
        with ExitStack() as s1c:
            o_hi = sb("o_hi", [P, HEADS, S], F32R, scope=s1c)
            o_lo = sb("o_lo", [P, HEADS, S], F32R, scope=s1c)
            prob = [sb(f"prob{n}", [P, PCOLS], scope=s1c) for n in range(2)]
            prob_t = sb("prob_t", [P, 2, TRI], scope=s1c)
            prob_ct = sb("prob_ct", [NC, S], scope=s1c)
            bias_g = sb("bias_g", [P, HPG, S + TT * NC], scope=s1c)
            top = sb("top", [P, 3, TT], scope=s1c)
            ntop = sb("ntop", [P, 3, TT], scope=s1c)
            total = [sb(f"total{n}", [P, 3, TT], scope=s1c) for n in range(2)]
            share = [sb(f"share{n}", [P, 3, TT], scope=s1c) for n in range(2)]
    with ExitStack() as s2:
        f_hi = sb("f_hi", [P, FKT, S], F32R, scope=s2)
        f_lo = sb("f_lo", [P, FKT, S], F32R, scope=s2)
        f_a = sb("f_a", [P, FT, S], scope=s2)
        f_b = sb("f_b", [P, FT, S], scope=s2)
    with ExitStack() as s3:
        ya_hi = sb("ya_hi", [P, KT, S], F32R, scope=s3)
        ya_lo = sb("ya_lo", [P, KT, S], F32R, scope=s3)
        yb_hi = sb("yb_hi", [P, 2 * len(POOLS), S], F32R, scope=s3)
        yb_lo = sb("yb_lo", [P, 2 * len(POOLS), S], F32R, scope=s3)
        with ExitStack() as s3a:
            cur = sb("cur", [P, CUR], scope=s3a)
            decay = sb("decay", [P, MH, TRI], scope=s3a)
            emm = sb("emm", [P, TT, MH], scope=s3a)
            cq = sb("cq", [P, FT, S + 3], scope=s3a)
            qm = sb("qm", [P, FT, S], scope=s3a)
            km = sb("km", [P, FT, S], scope=s3a)
            vm = sb("vm", [P, TT, BLK], scope=s3a)
            oz = sb("oz", [P, FT, S], scope=s3a)
            t1 = sb("t1", [P, FT, S], scope=s3a)
            t2 = sb("t2", [P, FT, S], scope=s3a)
            pm = sb("pm", [P, TRI], scope=s3a)
            pm_t = sb("pm_t", [P, TRI], scope=s3a)
            den = sb("den", [P, 2, TT], scope=s3a)
            g_fm = sb("g_fm", [2 * MH, S], scope=s3a)
            g_pre = sb("g_pre", [P, TT, 2 * MH], scope=s3a)
            g_bias = sb("g_bias", [P, 2 * MH], scope=s3a)
            g_t = sb("g_t", [P, 3, TT, MH], scope=s3a)
            g_max = sb("g_max", [P, MH, TT], scope=s3a)
            dec = sq[:, 0:3, :].rearrange("p a b -> p (a b)").rearrange("p (n c) -> p n c", n=2)
            hn = cq[:, :, 3:S + 3]
        with ExitStack() as s3b:
            m_hi = sb("m_hi", [P, KT, S], F32R, scope=s3b)
            m_lo = sb("m_lo", [P, KT, S], F32R, scope=s3b)
            m_a = sb("m_a", [P, FT, S], scope=s3b)
            m_b = sb("m_b", [P, FT, S], scope=s3b)
            m_t = sb("m_t", [P, FT, S], scope=s3b)
    with ExitStack() as s4:
        out_t = sb("out_t", [P, KT, S], scope=s4)
        y_t = sb("y_t", [P, KT, S], scope=s4)
    sel = oz[0:MH, :, :].rearrange("p a b -> p (a b)")
    causal = vm[:, 0, 0:TRI]
    tri = vm[:, 1, 0:P]
    g_row = vm[0:MH, 1, P:P + S]

    sets = [ctx.enter_context(nc.psum_tensor(f"set{n}", [P, 2 * BLK], F32)) for n in range(2)]
    m = [ctx.enter_context(nc.psum_tensor(f"misc{n}", [P, BLK], F32)) for n in range(4)]
    u_dram = nc.dram_tensor("u_dram", [HEADS, 2 * S], F32, kind="Internal").ap()

    raw_ready = [sem(f"raw_ready{n}") for n in range(RING)]
    hi_ready, lo_ready = sem("hi_ready"), sem("lo_ready")
    chunks_done = sem("chunks_done")
    taken = sem("taken")
    x_in = [sem(f"x_in{n}") for n in range(4)]
    gains_in, small_in = sem("gains_in"), sem("small_in")
    consts, ones_ready = sem("consts"), sem("ones_ready")
    dve_own, act_own, pool_own = sem("dve_own"), sem("act_own"), sem("pool_own")
    xh_ready, x_ready = sem("xh_ready"), sem("x_ready")
    hg_ready = sem("hg_ready")
    stats_ready, stats_sum = sem("stats_ready"), sem("stats_sum")
    var_ready, rms_ready = sem("var_ready"), sem("rms_ready")
    rel_done, u_ready, u_out, bias_in = sem("rel_done"), sem("u_ready"), sem("u_out"), sem("bias_in")
    gates_sig, gates_done, gates_ready = sem("gates_sig"), sem("gates_done"), sem("gates_ready")
    blk_in_ready, blk_h_ready, blk_ready = sem("blk_in_ready"), sem("blk_h_ready"), sem("blk_ready")
    hid_ready, hid_done, hid_copied, kvc_sum, kvc_ready = sem("hid_ready"), sem("hid_done"), sem("hid_copied"), sem("kvc_sum"), sem("kvc_ready")
    vg_ready, bg_in = sem("vg_ready"), sem("bg_in")
    scores_done, masked, exps_done = sem("scores_done"), sem("masked"), sem("exps_done")
    share_ready, probs_ready = sem("share_ready"), sem("probs_ready")
    pt_done, pt_ready, o_done, o_ready = sem("pt_done"), sem("pt_ready"), sem("o_done"), sem("o_ready")
    up_sig, up_prod, fh_ready, f_ready = sem("up_sig"), sem("up_prod"), sem("fh_ready"), sem("f_ready")
    cur_in, cur_free, decay_in = sem("cur_in"), sem("cur_free"), sem("decay_in")
    z_sig, pool_done, pool_ready, mix_done = sem("z_sig"), sem("pool_done"), sem("pool_ready"), sem("mix_done")
    yb_made, ybh_ready, yb_ready = sem("yb_made"), sem("ybh_ready"), sem("yb_ready")
    conv_ready, conv_sig, qkv_ready = sem("conv_ready"), sem("conv_sig"), sem("qkv_ready")
    gt_done, g2_pre, g2_log, g2_f, f_done, g_ready, g_row_done, g_row_ready, g_bc_done, decay_arg, decay_ready = (
        sem("gt_done"), sem("g2_pre"), sem("g2_log"), sem("g2_f"), sem("f_done"), sem("g_ready"), sem("g_row_done"),
        sem("g_row_ready"), sem("g_bc_done"), sem("decay_arg"), sem("decay_ready"))
    ms_done, mp_ready, mpt_done, mpt_ready = sem("ms_done"), sem("mp_ready"), sem("mpt_done"), sem("mpt_ready")
    mh_sum = sem("mh_sum")
    mh_done, mh_ready, mh_sq, mn_done = sem("mh_done"), sem("mh_ready"), sem("mh_sq"), sem("mn_done")
    dec_ready = sem("dec_ready")
    mn_var, mn_root, o_sig, zg_sig = sem("mn_var"), sem("mn_root"), sem("o_sig"), sem("zg_sig")
    ya_made, yah_ready, ya_ready = sem("ya_made"), sem("yah_ready"), sem("ya_ready")
    ga_sig, gb_sig, mg_made, mh2_ready, m_ready = (
        sem("ga_sig"), sem("gb_sig"), sem("mg_made"), sem("mh2_ready"), sem("m_ready"))
    y_ready, y2_ready, y_out = sem("y_ready"), sem("y2_ready"), sem("y_out")
    out_sq, y_scaled = sem("out_sq"), sem("y_scaled")

    def row(n):
        return rms[:, n, 0:S]

    def rows(n, count=FT):
        return row(n).unsqueeze(1).to_broadcast([P, count, S])

    def col(n, t):
        return rms[:, n, S + t:S + t + 1]

    def flat(ap):
        return ap.rearrange("p a b -> p (a b)")

    block = ctx.enter_context(nc.Block())

    def ml_block(i, b):
        if isinstance(i, int) and i == 0 and b == 0:
            return Pos(C_ML), B_ML
        number = B_ML + 1 + b
        return Pos(C_ML + 1 + b * NB, i, NML), (number + 6 * i if isinstance(i, int) else i * 6 + number)

    def ml_set(i, b):
        return (B_ML + (0 if isinstance(i, int) and i == 0 and b == 0 else 1) + b) % 2

    @block.sync
    def _(sp):
        def load(c, slot):
            sp.dma_start(raw[slot][:, :], d["weights"][c]).then_inc(raw_ready[slot], 16)

        def load_x(n):
            sp.dma_start(h[:, 4 * n:4 * n + 4, :],
                         d["x"][4 * n:4 * n + 4].rearrange("k p s -> p k s")).then_inc(x_in[n], 16)

        load(0, 0)
        load_x(0)
        load_x(1)
        load(1, 1)
        load_x(2)
        load(2, 2)
        load_x(3)
        load(3, 3)
        with sp.Fori(1, CHUNKS // RING) as i:
            for n in range(RING):
                sp.wait_ge(lo_ready, i * RING + (n - RING + 1))
                load(i * RING + n, n)
        for c in range(CHUNKS // RING * RING, CHUNKS):
            sp.wait_ge(lo_ready, c - RING + 1)
            load(c, c % RING)
        for n, ready, count in ((0, y_ready, 1), (1, y_ready, 2), (2, y2_ready, 1), (3, y_ready, 3)):
            sp.wait_ge(ready, count)
            sp.dma_start(d["out"][4 * n:4 * n + 4].rearrange("k p s -> p k s"),
                         y_t[:, 4 * n:4 * n + 4, :]).then_inc(y_out, 16)
        sp.wait_ge(y_out, 64)

    @block.gpsimd
    def _(pool):
        own = Chain(pool, pool_own)
        g = nc.gpsimd

        pool.dma_start(gains[:, :, :], d["gains"]).then_inc(gains_in, 16)
        for dst, name in ((rel[0:BUCKETS, :], "rel"), (ohd[:, :], "ohd"),
                          (w2[:, :, :, :], "w2"), (pos[:, :, :], "pos"), (valid[:, :], "valid")):
            pool.dma_start(dst, d[name]).then_inc(small_in, 16)
        own.link(g.memset(rel[BUCKETS:BUCKETS + 1, :], 1.0))
        own.link(g.memset(ident[:, :], 0.0))
        g.affine_select(out=ident[:, :], in_=ident[:, :], compare_op=ALU.not_equal, fill=1.0, base=0,
                        pattern=[[-1, P]], channel_multiplier=1).then_inc(consts, 1)

        def squares(src, k, first):
            own.link(g.tensor_tensor(sq[:, :, :], src, src, ALU.mult))
            own.link(g.tensor_tensor(sq[:, 0:2, :], sq[:, 0:2, :], sq[:, 2:4, :], ALU.add))
            if first:
                last = g.tensor_tensor(stat[:, k, :], sq[:, 0, :], sq[:, 1, :], ALU.add)
            else:
                own.link(g.tensor_tensor(sq[:, 0, :], sq[:, 0, :], sq[:, 1, :], ALU.add))
                last = g.tensor_tensor(stat[:, k, :], stat[:, k, :], sq[:, 0, :], ALU.add)
            last.then_inc(stats_ready, 1)

        for n in range(4):
            pool.wait_ge(x_in[n], 16)
            if n:
                pool.wait_ge(stats_ready, n)
            squares(h[:, 4 * n:4 * n + 4, :], 0, n == 0)

        pool.wait_ge(u_ready, 1)
        pool.dma_start(u_dram, u_row[:, :]).then_inc(u_out, 16)
        pool.wait_ge(u_out, 16)
        pool.dma_start(bias[:, :, 0:S], bass.AP(tensor=u_dram.tensor, offset=0,
                                              ap=[[1, P], [2 * S, HEADS], [1, S]])).then_inc(bias_in, 16)

        pool.wait_ge(bias_in, 16)
        near = (S - (CB - 1) - P + CS - 1) // CS
        g.tensor_copy(bias[:, :, S:S + near], bias[:, :, P + CB - 1:S:CS])
        g.memset(bias[:, :, S + near:S + NC], NEG)
        own.link(g.tensor_copy(bias[:, :, S + NC:S + 2 * NC], bias[:, :, CB - 1:S:CS]))

        def load_bias(gi):
            pool.dma_start(bias_g[:, :, :], bias[:, bass.ds(gi * HPG, HPG), :]).then_inc(bg_in, 16)

        def group(gi, first=False, last_group=False):
            for n in range(HPG):
                if n == 1:
                    if not first:
                        pool.wait_ge(o_done, gi * HPG)
                    for b in range(2):
                        g.tensor_copy(v_g[:, b, :, :], v_sw[:, b, :, bass.ds(gi * DH, DH)])
                    g.tensor_copy(v_cg[:, :], v_c[:, gi, :]).then_inc(vg_ready, 1)
                if n == HPG - 1 and not last_group:
                    pool.wait_ge(masked, gi * HPG + HPG)
                    load_bias(gi + 1)
                pool.wait_ge(share_ready, gi * HPG + (n + 1))
                pr, sh = prob[n % 2], share[n % 2]
                for b, t, lo, w in ((1, 0, O_SEL, P), (1, 1, O_SEL + P, S), (0, 0, O_CMP, NC),
                                    (0, 1, O_CMP + 16, NC), (2, 0, O_WIN, P), (2, 1, O_WIN + P, S)):
                    last = g.tensor_tensor(pr[:, lo:lo + w], pr[:, lo:lo + w],
                                           sh[:, b, t:t + 1].to_broadcast([P, w]), ALU.mult)
                last.then_inc(probs_ready, 1)

        pool.wait_ge(taken, B_G1)
        pool.wait_ge(kvc_ready, 1)
        load_bias(0)
        group(0, first=True)
        with pool.Fori(1, GROUPS - 1) as gi:
            group(gi)
        group(GROUPS - 1, last_group=True)

        pool.wait_ge(taken, B_OUT + 1)
        pool.wait_ge(rms_ready, 1)
        squares(h[:, 0:4, :], 0, True)
        with own.loop(1, 4, 3) as n:
            pool.wait_ge(taken, n + (B_OUT + 1))
            pool.wait_ge(stats_ready, n + 4)
            squares(h[:, bass.ds(n * 4, 4), :], 0, False)

        pool.wait_ge(rms_ready, 2)
        pool.wait_ge(hg_ready, 1)
        squares(h[:, 0:4, :], 0, True)
        pool.wait_ge(stats_ready, 9)
        squares(f_a[:, :, :], 1, True)
        with own.loop(1, 4, 6) as n:
            pool.wait_ge(hg_ready, n + 1)
            pool.wait_ge(stats_ready, n * 2 + 8)
            squares(h[:, bass.ds(n * 4, 4), :], 0, False)
            pool.wait_ge(stats_ready, n * 2 + 9)
            squares(f_a[:, :, :], 1, False)

        pool.wait_ge(chunks_done, C_ML)
        for dst, name in ((sel, "sel"), (causal, "causal"), (tri, "tri"), (g_bias[:, :], "g_bias")):
            pool.dma_start(dst, d[name]).then_inc(decay_in, 16)
        pool.dma_start(cur[:, :], d["cur"][0]).then_inc(cur_in, 16)
        pool.wait_ge(decay_ready, MH // 2)
        g.tensor_copy(dec[:, :, :], decay[:, 0:2, :]).then_inc(dec_ready, 1)
        with pool.Fori(1, 4) as i:
            pool.wait_ge(cur_free, i)
            g.tensor_copy(dec[:, :, :], decay[:, bass.ds(i * 2, 2), :]).then_inc(dec_ready, 1)
            pool.dma_start(cur[:, :], d["cur"][i]).then_inc(cur_in, 16)

        pool.wait_ge(taken, B_WO + 1)
        pool.wait_ge(rms_ready, 4)
        squares(out_t[:, 0:4, :], 0, True)
        with own.loop(1, 3, 3) as n:
            pool.wait_ge(taken, n + (B_WO + 1))
            pool.wait_ge(stats_ready, n + 16)
            squares(out_t[:, bass.ds(n * 4, 4), :], 0, False)

        pool.wait_ge(rms_ready, 5)
        pool.wait_ge(y_scaled, 3)
        part = y_t[:, 2 * FT:3 * FT, :]
        own.link(g.tensor_tensor(part, part, rows(POST), ALU.mult))
        g.tensor_tensor(part, part, h[:, 2 * FT:3 * FT, :], ALU.add).then_inc(y2_ready, 1)

    @block.scalar
    def _(act):
        own = Chain(act, act_own)
        a = nc.scalar.activation

        def split(at, j):
            if not at.exists(j):
                return
            act.wait_ge(raw_ready[at.slot(j)], (at.lap(j) + 1) * 16)
            if at.after_first_lap(j):
                act.wait_ge(chunks_done, at.at(j) - (RING - 1))
            a(w_hi[at.slot(j)][:, :], raw[at.slot(j)][:, :], ACT.Copy).then_inc(hi_ready, 1)

        def splits(at, count, extras=None):
            for j in range(count):
                split(at, j + AHEAD)
                if extras and j in extras:
                    extras[j]()

        def operand(kt, n):
            gain = gain2[:, kt] if n is None else gains[:, n, kt]
            a(x_hi[:, kt, :], h[:, kt, :], ACT.Copy, scale=gain).then_inc(xh_ready, 1)

        def root(n, count):
            act.wait_ge(var_ready, count)
            a(rms[:, n, :], rtmp[:, :], ACT.Sqrt).then_inc(rms_ready, 1)

        start = Pos(C_KV)
        act.wait_ge(gains_in, 16)
        split(start, 0)
        for n in range(4):
            act.wait_ge(x_in[n], 16)
            for kt in range(4 * n, 4 * n + 4):
                operand(bass.ds(kt, 1), MIX)
                if kt % 4 == 1 and n + 1 < AHEAD:
                    split(start, n + 1)

        splits(Pos(C_KV), NB, {7: lambda: root(MIX, 1)})
        splits(Pos(C_KV + NB), NB)
        for n in range(2):

            def blk_high(n=n):
                act.wait_ge(blk_in_ready, 2 * n + 2)
                a(blk_hi[:, n, :, :].rearrange("p l c -> p (l c)"),
                  blk_in[:, :, :, :].rearrange("p l g c -> p (l g c)"), ACT.Copy).then_inc(blk_h_ready, 1)

            splits(Pos(C_KV + 2 * NB, n, NB), NB, {2: blk_high})
        for n in range(2):
            splits(Pos(C_KV + 4 * NB, n, NB), NB)

        def gate_sigmoid():
            act.wait_ge(taken, B_G1 + 1)
            a(g_sig[:, :], g_sig[:, :], ACT.Sigmoid).then_inc(gates_sig, 1)

        splits(Pos(C_G1), 1)
        gate_sigmoid()
        for n in range(2):
            splits(Pos(C_CMP + n * NB), NB)
            act.wait_ge(taken, B_CMP + n + 1)
            a(hid_in[:, n, :], hid_in[:, n, :], ACT.Gelu_apprx_tanh).then_inc(hid_ready, 1)

        def exps(gi, n):
            act.wait_ge(masked, gi * HPG + (n + 1))
            pr = prob[n % 2]
            for b, t, lo, w in ((1, 0, O_SEL, P), (1, 1, O_SEL + P, S), (0, 0, O_CMP, NC),
                                (0, 1, O_CMP + 16, NC), (2, 0, O_WIN, P), (2, 1, O_WIN + P, S)):
                last = a(pr[:, lo:lo + w], pr[:, lo:lo + w], ACT.Exp, bias=ntop[:, b, t:t + 1],
                         accum_out=total[n % 2][:, b, t:t + 1])
            last.then_inc(exps_done, 1)

        def take_pt(gi, n):
            act.wait_ge(pt_done, gi * HPG + (n + 1))
            if real(gi, n - 1):
                act.wait_ge(o_done, gi * HPG + n)
            a(prob_t[:, 0, :], m[2][:, 0:TRI], ACT.Copy)
            a(prob_ct[:, 0:P], m[2][0:NC, TRI:BLK], ACT.Copy)
            a(prob_t[:, 1, :], m[3][:, 0:TRI], ACT.Copy)
            a(prob_ct[:, P:S], m[3][0:NC, TRI:BLK], ACT.Copy).then_inc(pt_ready, 1)

        def attention(gi, slot):
            n = slot // 2
            if slot % 2 == 0:
                if real(gi, n - 2):
                    take_pt(gi, n - 2)
                if real(gi, n - 1):
                    exps(gi, n - 1)

        def attentions(gi, slots=NB):
            return {s: lambda s=s: attention(gi, s) for s in range(slots)}

        splits(Pos(C_Q), NB)
        splits(Pos(C_Q + NB), NB, attentions(0))
        with act.Fori(1, GROUPS - 1) as gi:
            splits(Pos(C_Q + NB, gi, NB), NB, attentions(gi))

        def out_operand(n):
            for f in range(FT):
                act.wait_ge(taken, n + (B_OUT + 1))
                operand(bass.ds(n * FT + f, 1), FFN)

        splits(Pos(C_OUT), 2 * NB, attentions(3, ATT_SLOTS + 1) | {14: lambda: out_operand(0)})
        out_operand(1)
        with act.Fori(2, 4) as n:
            splits(Pos(C_OUT, n, NB), NB)
            out_operand(n)

        def up(i, first):
            splits(Pos(C_UP, i, 2 * NB), NB, {5: lambda: root(FFN, 2)} if first else None)
            act.wait_ge(taken, i * 2 + (B_UP + 1))
            a(f_b[:, :, :], f_a[:, :, :], ACT.Sigmoid).then_inc(up_sig, 1)
            splits(Pos(C_UP + NB, i, 2 * NB), NB)
            act.wait_ge(up_prod, i + 1)
            a(f_hi[:, bass.ds(i * FT, FT), :], f_b[:, :, :], ACT.Copy).then_inc(fh_ready, 1)

        up(0, True)
        with act.Fori(1, NUP) as i:
            up(i, False)

        with act.Fori(0, 2) as i:
            for b in range(2):
                splits(Pos(C_DOWN + b * ND, i, 2 * ND), ND)
                act.wait_ge(taken, i * 2 + (B_DOWN + b + 1))
                for f in range(FT):
                    operand(bass.ds(i * (2 * FT) + (b * FT + f), 1), None)

        def zg_sigmoid(i):
            act.wait_ge(taken, i * 6 + (B_ML + 7))
            a(t2[:, :, :], t1[:, :, :], ACT.Sigmoid).then_inc(zg_sig, 1)

        def ya_high(i):
            act.wait_ge(ya_made, i + 1)
            a(ya_hi[:, bass.ds(i * FT, FT), :], hn, ACT.Copy).then_inc(yah_ready, 1)

        def mlstm(i, first):
            splits(ml_block(i, 0)[0], NB, {6: lambda: root(FINAL, 3)} if first else
                   {0: lambda: zg_sigmoid(i - 1), 2: lambda: ya_high(i - 1)})
            if first:
                root(PRE, 4)
            act.wait_ge(taken, ml_block(i, 0)[1] + 1)
            a(t2[:, 0:2, :], t1[:, 2:4, :], ACT.Sigmoid).then_inc(z_sig, 1)
            if first:
                splits(Pos(C_ML + NB), 1)

            def softplus():
                act.wait_ge(g2_pre, 1)
                own.link(a(g_t[:, 1, :, :], g_t[:, 0, :, :], ACT.Exp))
                a(g_t[:, 1, :, :], g_t[:, 1, :, :], ACT.Ln, bias=1.0).then_inc(g2_log, 1)

            def yb_high():
                act.wait_ge(yb_made, i + 1)
                a(yb_hi[:, bass.ds(i * 2, 2), :], t2[:, 2:4, :], ACT.Copy).then_inc(ybh_ready, 1)

            def conv_sigmoid(n):
                act.wait_ge(conv_ready, i * 2 + (n + 1))
                a(t2[:, :, :], t1[:, :, :], ACT.Sigmoid).then_inc(conv_sig, 1)

            def decays(pair):
                act.wait_ge(decay_arg, 1)
                for k in (2 * pair, 2 * pair + 1):
                    for t in range(TT):
                        part = decay[:, k, t * P:(t + 1) * P + t * P]
                        last = a(part, part, ACT.Exp, bias=g_max[:, k, t:t + 1])
                if pair == MH // 2 - 1:
                    last = a(emm[:, :, :], emm[:, :, :], ACT.Exp)
                last.then_inc(decay_ready, 1)

            splits(ml_block(i, 1)[0], NB, {5: yb_high} | ({2: softplus} if first else {}))
            splits(ml_block(i, 2)[0], NB, {4: lambda: conv_sigmoid(0)})
            decay_steps = {k: lambda k=k: decays(k) for k in range(MH // 2)} if first else {}
            splits(ml_block(i, 3)[0], NB, {4: lambda: conv_sigmoid(1)} | decay_steps)

            def take_pmt(n):
                act.wait_ge(mpt_done, i * 2 + (n + 1))
                a(pm_t[:, :], m[1][:, 0:TRI], ACT.Copy).then_inc(mpt_ready, 1)

            def square(n):
                act.wait_ge(mh_ready, i * 2 + (n + 1))
                a(t2[:, 2 * n:2 * n + 2, :], hn[:, 2 * n:2 * n + 2, :], ACT.Square).then_inc(mh_sq, 1)

            def head_root(n):
                act.wait_ge(mn_var, i * 2 + (n + 1))
                a(t1[:, 2 + n, :], t1[:, n, :], ACT.Sqrt).then_inc(mn_root, 1)

            splits(ml_block(i, 4)[0], NB, {4: lambda: take_pmt(0), 6: lambda: square(0)})
            act.wait_ge(taken, ml_block(i, 4)[1] + 1)
            a(oz[:, :, :], t1[:, :, :], ACT.Sigmoid).then_inc(o_sig, 1)
            splits(ml_block(i, 5)[0], NB, {0: lambda: take_pmt(1), 3: lambda: square(1), 4: lambda: head_root(0),
                                           6: lambda: head_root(1)})

        mlstm(0, True)
        with act.Fori(1, 4) as i:
            mlstm(i, False)

        def merge(i, extras=None):
            splits(Pos(C_MG, i, NMG), NB, extras)
            act.wait_ge(taken, i * 4 + (B_MG + 1))
            a(m_a[:, :, :], m_a[:, :, :], ACT.Sigmoid).then_inc(ga_sig, 1)
            splits(Pos(C_MG + NB, i, NMG), NB)
            act.wait_ge(taken, i * 4 + (B_MG + 2))
            a(m_b[:, :, :], m_b[:, :, :], ACT.Sigmoid).then_inc(gb_sig, 1)
            splits(Pos(C_MG + 2 * NB, i, NMG), NB)
            splits(Pos(C_MG + 3 * NB, i, NMG), NB // 2)
            act.wait_ge(mg_made, i + 1)
            a(m_hi[:, bass.ds(i * FT, FT), :], m_t[:, :, :], ACT.Copy).then_inc(mh2_ready, 1)

        merge(0, {0: lambda: zg_sigmoid(3), 2: lambda: ya_high(3)})
        with act.Fori(1, 4) as i:
            merge(i)

        def scale_y(n):
            act.wait_ge(taken, B_WO + n + 1)
            for kt in range(n * FT, (n + 1) * FT):
                last = a(y_t[:, kt, :], out_t[:, kt, :], ACT.Copy, scale=gains[:, POST, kt:kt + 1])
            last.then_inc(y_scaled, 1)

        for n in range(4):
            splits(Pos(C_WO + n * NB), NB, {2: lambda n=n: scale_y(n - 1)} if n else None)
        act.wait_ge(stats_ready, 19)
        for k in range(2):
            act.wait_ge(taken, B_WO + 4 + k)
            a(sq[:, 2 * k:2 * k + 2, :], out_t[:, 3 * FT + 2 * k:3 * FT + 2 * k + 2, :], ACT.Square).then_inc(out_sq, 1)
        root(POST, 5)
        scale_y(3)

    @block.vector
    def _(dve):
        own = Chain(dve, dve_own)
        v = nc.vector
        tt, stt = v.tensor_tensor, v.scalar_tensor_tensor

        def split(at, j):
            if not at.exists(j):
                return
            dve.wait_ge(hi_ready, at.at(j) + 1)
            s = at.slot(j)
            tt(w_lo[s][:, :], raw[s][:, :], w_hi[s][:, :].bitcast(F32), ALU.subtract).then_inc(lo_ready, 1)

        def splits(at, count, extras=None, urgent=None):
            for j in range(count):
                if urgent and j in urgent:
                    urgent[j]()
                split(at, j + AHEAD)
                if extras and j in extras:
                    extras[j]()
            dve.wait_ge(chunks_done, at.at(count))

        def psum(number):
            return sets[number % 2][:, :].rearrange("p (f s) -> p f s", f=FT)

        def operand(kt, n, count):
            gain = gain2[:, kt] if n is None else gains[:, n, kt]
            dve.wait_ge(xh_ready, count)
            stt(x_lo[:, kt, :], h[:, kt, :], gain, x_hi[:, kt, :].bitcast(F32),
                ALU.mult, ALU.subtract).then_inc(x_ready, 1)

        def variance(count, bank=0, width=S + TT):
            dve.wait_ge(stats_sum, count)
            own.link(v.tensor_scalar(rtmp[:, 0:width], m[bank][:, 0:width], 1.0 / D, EPS, ALU.mult, ALU.add))
            v.reciprocal(rtmp[:, 0:width], rtmp[:, 0:width]).then_inc(var_ready, 1)

        v.memset(ones[:, :], 1.0).then_inc(ones_ready, 1)

        start = Pos(C_KV)
        dve.wait_ge(gains_in, 16)
        tt(gain2[:, :], gains[:, FINAL, :], gains[:, PRE, :], ALU.mult)
        split(start, 0)
        for n in range(4):
            for kt in range(4 * n, 4 * n + 4):
                operand(bass.ds(kt, 1), MIX, kt + 1)
                if kt % 4 == 1 and n + 1 < AHEAD:
                    split(start, n + 1)

        def take(number, dst, norm, scale=None):
            if scale is None:
                tt(dst, psum(number), rows(norm), ALU.mult).then_inc(taken, 1)
            else:
                stt(dst, psum(number), scale, rows(norm), ALU.mult, ALU.mult).then_inc(taken, 1)

        def take_tokens(number, dsts, norm, width=BLK):
            for t in range(TT):
                last = v.tensor_scalar(dsts[t], sets[number % 2][:, t * width:t * width + dsts[t].shape[-1]],
                                       col(norm, t), None, ALU.mult)
            last.then_inc(taken, 1)

        def relative():
            dve.wait_ge(rel_done, 1)
            v.tensor_copy(u_row[:, :], m[3][0:HEADS, :]).then_inc(u_ready, 1)

        splits(Pos(C_KV), NB, {2: relative, 7: lambda: variance(1)})
        dve.wait_ge(rms_ready, 1)
        dve.wait_ge(u_out, 16)
        take(B_KV, kv_c[:, 0, :, :], MIX)
        splits(Pos(C_KV + NB), NB)
        take(B_KV + 1, kv_c[:, 1, :, :], MIX)
        for n in range(2):

            def blk_input(n=n):
                dve.wait_ge(taken, B_KV + n + 1)
                if n == 0:
                    dve.wait_ge(small_in, 80)
                for half in range(2):
                    src = kv_c[:, n, :, :].rearrange("p g (c l) -> p l g c", l=CS)[:, :, :, half:half + NC]
                    tt(blk_in[:, half * CS:(half + 1) * CS, :, :], src,
                       pos[:, n, half * CS:(half + 1) * CS].unsqueeze(2).unsqueeze(3)
                       .to_broadcast([P, CS, GROUPS, NC]), ALU.add).then_inc(blk_in_ready, 1)

            def blk_low(n=n):
                dve.wait_ge(blk_h_ready, n + 1)
                tt(blk_lo[:, n, :, :].rearrange("p l c -> p (l c)"),
                   blk_in[:, :, :, :].rearrange("p l g c -> p (l g c)"),
                   blk_hi[:, n, :, :].rearrange("p l c -> p (l c)").bitcast(F32),
                   ALU.subtract).then_inc(blk_ready, 1)

            splits(Pos(C_KV + (2 + n) * NB), NB, {1: blk_input, 3: blk_low})
            take(B_KV + 2 + n, k_sw[:, n, :, :], MIX)
        for n in range(2):
            splits(Pos(C_KV + (4 + n) * NB), NB)
            take_tokens(B_KV + 4 + n, [v_sw[:, n, t, :] for t in range(TT)], MIX)
        splits(Pos(C_G1), 1)
        tt(g_sig[:, ::-1], sets[B_G1 % 2][0:3 * HEADS, 0:S], rms[0:3 * HEADS, MIX, 0:S], ALU.mult).then_inc(taken, 1)

        def gates_out():
            dve.wait_ge(gates_done, 1)
            for t in range(TT):
                last = v.tensor_copy(gate[:, :, :, t],
                                     m[0][:, t * 48:(t + 1) * 48].rearrange("p (b h) -> p h b", b=3))
            own.link(last)
            tt(gate[:, :, 0, :], gate[:, :, 0, :], valid[:, :].unsqueeze(1).to_broadcast([P, HEADS, TT]),
               ALU.mult).then_inc(gates_ready, 1)

        for n in range(2):
            splits(Pos(C_CMP + n * NB), NB, {5: gates_out} if n == 0 else None)
            v.tensor_copy(hid_in[:, n, :], sets[(B_CMP + n) % 2][0:GROUPS * NC, 0:CH]).then_inc(taken, 1)

        def hidden():
            dve.wait_ge(hid_done, 1)
            v.tensor_copy(hid[:, :, :, :].rearrange("p n f c -> p (n f c)"),
                          m[2][:, 0:4 * GROUPS * NC]).then_inc(hid_copied, 1)

        def compressed():
            dve.wait_ge(kvc_sum, 1)
            v.tensor_copy(k_c[:, :, :].rearrange("p g c -> p (g c)"), m[0][:, 0:GROUPS * NC])
            v.tensor_copy(v_c[:, :, :].rearrange("p g d -> p (g d)"), m[1][0:NC, :]).then_inc(kvc_ready, 1)

        def mask_scores(gi, n):
            head = gi * HPG + n
            if n == 0:
                dve.wait_ge(bg_in, gi * 16 + 16)
            dve.wait_ge(scores_done, head + 1)
            if not (isinstance(gi, int) and gi * HPG + n < 2):
                dve.wait_ge(pt_done, head - 1)
            pr = prob[n % 2]
            pair = "p (t c) -> p t c"
            pr_c = pr[:, O_CMP:O_CMP + 32].rearrange(pair, t=TT)[:, :, 0:NC]
            tt(pr_c, m[0][:, TRI:TRI + 32].rearrange(pair, t=TT)[:, :, 0:NC], bias_g[:, n, S:].rearrange(pair, t=TT), ALU.add)
            for b, t, o, src, add in (
                    (1, 0, O_SEL, m[0][:, 0:P], bias_g[:, n, P:S]),
                    (1, 1, O_SEL + P, m[0][:, P:TRI], bias_g[:, n, 0:S]),
                    (2, 0, O_WIN, m[1][:, 0:P], bias_g[:, n, P:S]),
                    (2, 1, O_WIN + P, m[1][:, P:TRI], bias_g[:, n, 0:S])):
                last = v.tensor_tensor_reduce(out=pr[:, o:o + (t + 1) * P], in0=src, in1=add, scale=1.0,
                                              scalar=-3e38, op0=ALU.add, op1=ALU.max, accum_out=top[:, b, t:t + 1])
            own.link(last)
            last = v.tensor_reduce(top[:, 0, :], pr_c, mybir.AxisListType.X, ALU.max)
            own.link(last)
            v.tensor_scalar(flat(ntop[:, :, :]), flat(top[:, :, :]), -1.0, None, ALU.mult).then_inc(masked, 1)

        def make_share(gi, n):
            head = gi * HPG + n
            dve.wait_ge(exps_done, head + 1)
            if isinstance(gi, int) and head == 0:
                dve.wait_ge(gates_ready, 1)
            own.link(v.reciprocal(flat(total[n % 2][:, :, :]), flat(total[n % 2][:, :, :])))
            if not (isinstance(gi, int) and gi * HPG + n < 2):
                dve.wait_ge(probs_ready, head - 1)
            tt(share[n % 2][:, :, :], total[n % 2][:, :, :],
               gate[:, bass.ds(head, 1), :, :].rearrange("p a b t -> p (a b) t"), ALU.mult).then_inc(share_ready, 1)

        def take_head(gi, n):
            head = gi * HPG + n
            dve.wait_ge(o_done, head + 1)
            halves = "p (t s) -> p t s"
            src = m[1][:, 0:S].rearrange(halves, t=TT)[:, :, ::-1]
            high = o_hi[:, bass.ds(head, 1), :].rearrange("p a (t s) -> p (a t) s", t=TT)
            low = o_lo[:, bass.ds(head, 1), :].rearrange("p a (t s) -> p (a t) s", t=TT)
            own.link(v.tensor_copy(high, src))
            tt(low, src, high.bitcast(F32), ALU.subtract).then_inc(o_ready, 1)

        def heads_out(gi, slots=NB):
            return {2 * n: lambda n=n: take_head(gi, n - 3) for n in range((slots + 1) // 2) if real(gi, n - 3)}

        def softmax_step(gi, n):
            if real(gi, n - 1):
                make_share(gi, n - 1)
            if real(gi, n):
                mask_scores(gi, n)

        def softmaxes(gi, slots=NB):
            return {2 * n + 1: lambda n=n: softmax_step(gi, n) for n in range(slots // 2)}

        q_scale = DH ** -0.5
        splits(Pos(C_Q), NB, {3: hidden, 5: compressed})
        take(B_Q, q_t[:, :, ::-1], MIX, q_scale)
        splits(Pos(C_Q + NB), NB, heads_out(0), softmaxes(0))
        take(B_Q + 1, q_t[:, :, ::-1], MIX, q_scale)
        with own.loop(1, GROUPS - 1, 4 * HPG) as gi:
            splits(Pos(C_Q + NB, gi, NB), NB, heads_out(gi), softmaxes(gi))
            take(B_Q + 1, q_t[:, :, ::-1], MIX, q_scale)

        def out_block(number, n):
            kts = bass.ds(n * FT, FT)
            tt(h[:, kts, :], psum(number), h[:, kts, :], ALU.add).then_inc(taken, 1)
            dve.wait_ge(taken, n + (B_OUT + 1))
            for f in range(FT):
                operand(bass.ds(n * FT + f, 1), FFN, n * FT + (KT + f + 1))

        def first_out():
            dve.wait_ge(chunks_done, C_OUT + 14)
            out_block(B_OUT, 0)

        splits(Pos(C_OUT), 2 * NB, heads_out(3, ATT_SLOTS + 1) | {14: first_out}, softmaxes(3, ATT_SLOTS))
        out_block(B_OUT + 1, 1)
        for n in (2, 3):
            splits(Pos(C_OUT, n, NB), NB)
            out_block(B_OUT + n, n)

        def up(i, first):
            splits(Pos(C_UP, i, 2 * NB), NB, {4: lambda: variance(2)} if first else None)
            if first:
                dve.wait_ge(rms_ready, 2)
            take(B_UP, f_a[:, :, :], FFN)

            def gated():
                dve.wait_ge(up_sig, i + 1)
                own.link(tt(f_a[:, :, :], f_a[:, :, :], f_b[:, :, :], ALU.mult))

            splits(Pos(C_UP + NB, i, 2 * NB), NB, {1: gated})
            take(B_UP + 1, f_b[:, :, :], FFN)
            dve.wait_ge(taken, i * 2 + (B_UP + 2))
            tt(f_b[:, :, :], f_b[:, :, :], f_a[:, :, :], ALU.mult).then_inc(up_prod, 1)
            dve.wait_ge(fh_ready, i + 1)
            kts = bass.ds(i * FT, FT)
            tt(f_lo[:, kts, :], f_b[:, :, :], f_hi[:, kts, :].bitcast(F32), ALU.subtract).then_inc(f_ready, 1)

        up(0, True)
        with own.loop(1, NUP, 1) as i:
            up(i, False)

        def down(i, b):
            splits(Pos(C_DOWN + b * ND, i, 2 * ND), ND)
            kts = bass.ds(i * (2 * FT) + b * FT, FT)
            tt(h[:, kts, :], psum(B_DOWN + b), h[:, kts, :], ALU.add).then_inc(taken, 1)
            dve.wait_ge(taken, i * 2 + (B_DOWN + b + 1))
            dve.wait_ge(stats_ready, i * 4 + (8 + 2 * b))
            for f in range(FT):
                kt = bass.ds(i * (2 * FT) + (b * FT + f), 1)
                last = v.tensor_scalar(f_a[:, f, :], h[:, kt, :].rearrange("p a s -> p (a s)"),
                                       gains[:, FINAL, kt], None, ALU.mult)
            last.then_inc(hg_ready, 1)
            for f in range(FT):
                operand(bass.ds(i * (2 * FT) + (b * FT + f), 1), None, i * (2 * FT) + (2 * KT + b * FT + f + 1))

        with dve.Fori(0, 2) as i:
            down(i, 0)
            down(i, 1)

        def second_variance():
            dve.wait_ge(rms_ready, 3)
            own.link(tt(rtmp[:, :], rms[:, FINAL, :], rms[:, FINAL, :], ALU.mult))
            own.link(tt(rtmp[:, :], rtmp[:, :], m[1][:, 0:S + TT], ALU.mult))
            own.link(v.tensor_scalar(rtmp[:, :], rtmp[:, :], 1.0 / D, EPS, ALU.mult, ALU.add))
            v.reciprocal(rtmp[:, :], rtmp[:, :]).then_inc(var_ready, 1)

        def zg_times_z(i):
            dve.wait_ge(taken, i * 6 + (B_ML + 7))
            own.link(tt(hn, hn, t1[:, :, :], ALU.mult))

        def zg_times_sigmoid(i):
            dve.wait_ge(zg_sig, i + 1)
            tt(hn, hn, t2[:, :, :], ALU.mult).then_inc(ya_made, 1)

        def ya_low(i):
            dve.wait_ge(yah_ready, i + 1)
            kts = bass.ds(i * FT, FT)
            tt(ya_lo[:, kts, :], hn, ya_hi[:, kts, :].bitcast(F32), ALU.subtract).then_inc(ya_ready, 1)

        def mlstm(i, first):
            at, number = ml_block(i, 0)
            the_set = ml_set(i, 0)
            splits(at, NB, {6: lambda: variance(4), 7: second_variance} if first else
                   {0: lambda: zg_times_z(i - 1), 1: lambda: zg_times_sigmoid(i - 1), 3: lambda: ya_low(i - 1)})
            if first:
                dve.wait_ge(rms_ready, 4)
                own.link(tt(rms[:, PRE, :], rms[:, PRE, :], rms[:, FINAL, :], ALU.mult))
            for t in range(TT):
                v.tensor_scalar(t1[:, t, :], sets[the_set][:, t * PG:(t + 1) * PG], col(PRE, t), None, ALU.mult)
            tt(t1[:, 2:4, :], sets[the_set][:, BLK:].rearrange("p (f s) -> p f s", f=2), rows(PRE, 2),
               ALU.mult).then_inc(taken, 1)
            if first:
                splits(Pos(C_ML + NB), 1)
                tt(g_fm[:, :], sets[(B_ML + 1) % 2][0:2 * MH, 0:S], rms[0:2 * MH, PRE, 0:S], ALU.mult).then_inc(taken, 1)

            def z_silu():
                dve.wait_ge(z_sig, i + 1)
                own.link(tt(t1[:, 2:4, :], t1[:, 2:4, :], t2[:, 0:2, :], ALU.mult))

            def gate_inputs():
                dve.wait_ge(gt_done, 1)
                dve.wait_ge(decay_in, 64)
                own.link(tt(g_pre[:, :, :], m[3][:, 0:TT * 2 * MH].rearrange("p (t h) -> p t h", t=TT),
                            g_bias[:, :].unsqueeze(1).to_broadcast([P, TT, 2 * MH]), ALU.add))
                forget = g_pre[:, :, MH:2 * MH]
                stt(g_t[:, 0, :, :], forget, -1.0, forget, ALU.mult, ALU.min).then_inc(g2_pre, 1)

            def log_forget():
                dve.wait_ge(g2_log, 1)
                stt(g_t[:, 0, :, :], g_pre[:, :, MH:2 * MH], 0.0, g_t[:, 1, :, :], ALU.min, ALU.subtract).then_inc(g2_f, 1)

            def cumulated():
                dve.wait_ge(f_done, 1)
                sums = m[3][:, 0:TT * MH].rearrange("p (t h) -> p t h", t=TT)
                v.tensor_copy(g_t[:, 1, :, :], sums)
                tt(g_t[:, 2, :, :], g_pre[:, :, 0:MH], sums, ALU.subtract).then_inc(g_ready, 1)

            def row_copy():
                dve.wait_ge(g_row_done, 1)
                v.tensor_copy(g_row, m[2][0:MH, 0:S]).then_inc(g_row_ready, 1)

            def arguments(pair):
                dve.wait_ge(g_bc_done, 1)
                for k in (2 * pair, 2 * pair + 1):
                    src = m[pair][:, (k % 2) * S:(k % 2) * S + S]
                    for t in range(TT):
                        part = slice(t * P, (t + 1) * P + t * P)
                        last = v.tensor_tensor_reduce(out=decay[:, k, part], in0=src[:, 0:(t + 1) * P],
                                                      in1=causal[:, part], scale=1.0, scalar=0.0, op0=ALU.add,
                                                      op1=ALU.max, accum_out=g_max[:, k, t:t + 1])
                if pair == MH // 2 - 1:
                    own.link(last)
                    for t in range(TT):
                        last = stt(emm[:, t, :], g_max[:, :, t], -1.0, g_t[:, 1, t, :], ALU.mult, ALU.subtract)
                    own.link(last)
                    v.tensor_scalar(flat(g_max[:, :, :]), flat(g_max[:, :, :]), -1.0, None,
                                    ALU.mult).then_inc(decay_arg, 1)

            def take_pooled():
                dve.wait_ge(pool_done, i + 1)
                v.tensor_copy(flat(t2[:, 0:2, :]), m[0][:, :]).then_inc(pool_ready, 1)

            def take_mixed():
                dve.wait_ge(mix_done, i + 1)
                dve.wait_ge(cur_in, i * 16 + 16)
                for k in range(2):
                    last = stt(t2[:, 2 + k, :], m[1][:, k * S:(k + 1) * S], cur[:, P_SC + k:P_SC + k + 1],
                               t1[:, 2 + k, :], ALU.mult, ALU.mult)
                last.then_inc(yb_made, 1)

            def yb_low():
                dve.wait_ge(ybh_ready, i + 1)
                kts = bass.ds(i * 2, 2)
                tt(yb_lo[:, kts, :], t2[:, 2:4, :], yb_hi[:, kts, :].bitcast(F32), ALU.subtract).then_inc(yb_ready, 1)

            def take_conv_input(b):
                tt(cq[:, :, 3:S + 3], sets[ml_set(i, b)][:, :].rearrange("p (f s) -> p f s", f=FT), rows(PRE),
                   ALU.mult).then_inc(taken, 1)

            def convolve(b, params, k):
                if k == 0:
                    dve.wait_ge(taken, ml_block(i, b)[1] + 1)
                for f in range(FT):
                    c = params + 5 * f
                    if k == 0:
                        last = v.tensor_scalar(t1[:, f, :], cq[:, f, 0:S], cur[:, c:c + 1], cur[:, c + 4:c + 5],
                                               ALU.mult, ALU.add)
                    else:
                        last = stt(t1[:, f, :], cq[:, f, k:k + S], cur[:, c + k:c + k + 1], t1[:, f, :],
                                   ALU.mult, ALU.add)
                if k < 3:
                    own.link(last)
                else:
                    last.then_inc(conv_ready, 1)

            def silu(dst, b, scale):
                dve.wait_ge(conv_ready, i * 2 + (b + 1))
                dve.wait_ge(conv_sig, i * 2 + (b + 1))
                stt(dst, t1[:, :, :], scale, t2[:, :, :], ALU.mult, ALU.mult).then_inc(qkv_ready, 1)

            def together(*steps):
                return lambda: [step() for step in steps]

            if first:
                extras = {0: z_silu, 1: gate_inputs, 2: take_pooled, 3: log_forget, 4: together(take_mixed, cumulated),
                          6: together(yb_low, row_copy)}
            else:
                extras = {0: z_silu, 2: take_pooled, 4: take_mixed, 6: yb_low}
            splits(ml_block(i, 1)[0], NB, extras)
            take_conv_input(1)
            taps = {k: lambda k=k: convolve(1, Q_CONV, k) for k in range(4)}

            def q_silu():
                silu(qm[:, :, :], 0, MD ** -0.5)

            if first:
                args = [lambda k=k: arguments(k) for k in range(MH // 2)]
                extras = taps | {4: args[0], 5: together(q_silu, args[1]), 6: args[2], 7: args[3]}
            else:
                extras = taps | {5: q_silu}
            splits(ml_block(i, 2)[0], NB, extras)
            take_conv_input(2)
            taps = {k: lambda k=k: convolve(2, K_CONV, k) for k in range(4)}
            splits(ml_block(i, 3)[0], NB, taps | {5: lambda: silu(km[:, :, :], 1, 1.0)})
            for t in range(TT):
                last = v.tensor_scalar(vm[:, t, :], sets[ml_set(i, 3)][:, t * BLK:(t + 1) * BLK], col(PRE, t), None, ALU.mult)
            last.then_inc(taken, 1)

            def head_probs(n):
                dve.wait_ge(ms_done, i * 2 + (n + 1))
                if n == 0:
                    dve.wait_ge(dec_ready, i + 1)
                if not (first and n == 0):
                    dve.wait_ge(mpt_done, i * 2 + n)
                for t in range(TT):
                    part = slice(t * P, (t + 1) * P + t * P)
                    last = v.tensor_tensor_reduce(out=pm[:, part], in0=m[0][:, part], in1=dec[:, n, part], scale=1.0, scalar=0.0,
                                                  op0=ALU.mult, op1=ALU.add, accum_out=den[:, 0, t:t + 1])
                own.link(last)
                own.link(stt(den[:, 1, :], den[:, 0, :], -1.0, den[:, 0, :], ALU.mult, ALU.max))
                own.link(tt(den[:, 1, :], den[:, 1, :], emm[:, :, bass.ds(i * 2 + n, 1)].rearrange("p t a -> p (t a)"), ALU.max))
                own.link(v.reciprocal(den[:, 1, :], den[:, 1, :]))
                for t in range(TT):
                    part = slice(t * P, (t + 1) * P + t * P)
                    last = v.tensor_scalar(pm[:, part], pm[:, part], den[:, 1, t:t + 1], None, ALU.mult)
                last.then_inc(mp_ready, 1)

            def head_out(n):
                dve.wait_ge(mh_done, i * 2 + (n + 1))
                v.tensor_copy(hn[:, 2 * n:2 * n + 2, :], m[2][:, :].rearrange("p (a s) -> p a s", a=2)).then_inc(mh_ready, 1)

            def head_sum(n):
                dve.wait_ge(mh_sq, i * 2 + (n + 1))
                tt(t2[:, 2 * n, :], t2[:, 2 * n, :], t2[:, 2 * n + 1, :], ALU.add).then_inc(mh_sum, 1)

            def head_var(n):
                dve.wait_ge(mn_done, i * 2 + (n + 1))
                if n == 0:
                    dve.wait_ge(o_sig, i + 1)
                own.link(v.tensor_scalar(t1[:, n, :], m[3][:, 0:S], 1.0 / MD, EPS, ALU.mult, ALU.add))
                v.reciprocal(t1[:, n, :], t1[:, n, :]).then_inc(mn_var, 1)

            def head_norm(n):
                dve.wait_ge(mn_root, i * 2 + (n + 1))
                dve.wait_ge(mh_ready, i * 2 + (n + 1))
                for f in range(2 * n, 2 * n + 2):
                    last = stt(hn[:, f, :], hn[:, f, :], cur[:, N_W + f:N_W + f + 1], t1[:, 2 + n, :], ALU.mult, ALU.mult)
                if n == 0:
                    own.link(last)
                else:
                    last.then_inc(cur_free, 1)

            def gate_out():
                dve.wait_ge(cur_free, i + 1)
                dve.wait_ge(o_sig, i + 1)
                own.link(tt(hn, hn, oz[:, :, :], ALU.mult))

            splits(ml_block(i, 4)[0], NB, {2: lambda: head_probs(0), 5: lambda: head_out(0), 6: lambda: head_probs(1)})
            tt(t1[:, :, :], sets[ml_set(i, 4)][:, :].rearrange("p (f s) -> p f s", f=FT), rows(PRE), ALU.mult).then_inc(taken, 1)
            splits(ml_block(i, 5)[0], NB,
                   {0: lambda: head_sum(0), 2: lambda: head_out(1), 3: lambda: head_var(0), 4: lambda: head_sum(1),
                    5: lambda: head_norm(0), 6: lambda: head_var(1), 7: together(lambda: head_norm(1), gate_out)})
            tt(t1[:, :, :], sets[ml_set(i, 5)][:, :].rearrange("p (f s) -> p f s", f=FT), rows(PRE), ALU.mult).then_inc(taken, 1)

        v.memset(cq[:, :, 0:3], 0.0)
        mlstm(0, True)
        with own.loop(1, 4, ML_LINKS) as i:
            mlstm(i, False)

        def merge(i, extras=None):
            splits(Pos(C_MG, i, NMG), NB, extras)
            take(B_MG, m_a[:, :, :], PRE)
            splits(Pos(C_MG + NB, i, NMG), NB)
            take(B_MG + 1, m_b[:, :, :], PRE)
            splits(Pos(C_MG + 2 * NB, i, NMG), NB)
            dve.wait_ge(ga_sig, i + 1)
            tt(m_a[:, :, :], psum(B_MG + 2), m_a[:, :, :], ALU.mult).then_inc(taken, 1)
            splits(Pos(C_MG + 3 * NB, i, NMG), NB // 2)
            dve.wait_ge(gb_sig, i + 1)
            tt(m_b[:, :, :], psum(B_MG + 3), m_b[:, :, :], ALU.mult).then_inc(taken, 1)
            dve.wait_ge(taken, i * 4 + (B_MG + 4))
            tt(m_t[:, :, :], m_a[:, :, :], m_b[:, :, :], ALU.add).then_inc(mg_made, 1)
            dve.wait_ge(mh2_ready, i + 1)
            kts = bass.ds(i * FT, FT)
            tt(m_lo[:, kts, :], m_t[:, :, :], m_hi[:, kts, :].bitcast(F32), ALU.subtract).then_inc(m_ready, 1)

        merge(0, {0: lambda: zg_times_z(3), 1: lambda: zg_times_sigmoid(3), 3: lambda: ya_low(3)})
        with dve.Fori(1, 4) as i:
            merge(i)

        def out_taken(n):
            if n < 3:
                v.tensor_copy(out_t[:, n * FT:(n + 1) * FT, :], psum(B_WO + n)).then_inc(taken, 1)
            else:
                for k in range(2):
                    v.tensor_copy(out_t[:, n * FT + 2 * k:n * FT + 2 * k + 2, :],
                                  psum(B_WO + n)[:, 2 * k:2 * k + 2, :]).then_inc(taken, 1)

        def first_layer_out(kt):
            stt(h[:, kt, :], h[:, kt, :], gains[:, FINAL, kt:kt + 1], row(FINAL), ALU.mult, ALU.mult)

        for n in range(4):
            splits(Pos(C_WO + n * NB), NB, {j: lambda kt=n * FT + j: first_layer_out(kt) for j in range(FT)})
            out_taken(n)
        variance(5, width=S)
        dve.wait_ge(rms_ready, 5)
        for n in (0, 1, 3):
            dve.wait_ge(y_scaled, n + 1)
            part = y_t[:, n * FT:(n + 1) * FT, :]
            own.link(tt(part, part, rows(POST), ALU.mult))
            tt(part, part, h[:, n * FT:(n + 1) * FT, :], ALU.add).then_inc(y_ready, 1)

    @block.tensor
    def _(pe):
        mm = nc.tensor.matmul

        def await_set(number, same=False):
            if isinstance(number, int):
                if number - 1 + same > 0:
                    pe.wait_ge(taken, number - 1 + same)
            else:
                pe.wait_ge(taken, number + (same - 1))

        def features(at, j, out, hi, lo, kts, first, ft=FT, ft0=0):
            slot = at.slot(j)
            for k, kt in enumerate(kts):
                for f in range(ft):
                    c = k * BLK + (ft0 + f) * P
                    o = out[:, (ft0 + f) * S:(ft0 + f + 1) * S]
                    starts = first and k == 0 and f % 2 == 0
                    mm(o, w_hi[slot][:, c:c + P], hi[:, kt, :], start=starts, stop=False, skip_group_check=True)
                    mm(o, w_hi[slot][:, c:c + P], lo[:, kt, :], start=False, stop=False, skip_group_check=True)
                    last = mm(o, w_lo[slot][:, c:c + P], hi[:, kt, :], start=False, stop=True, skip_group_check=True)
            return last

        def tokens(at, j, out, hi, lo, kts, first, width, cols=0, per_k=BLK, pitch=BLK):
            slot = at.slot(j)
            for k, kt in enumerate(kts):
                for t in range(TT):
                    o = out[:, t * pitch:t * pitch + width]
                    c = k * per_k + cols
                    x = slice(t * P, (t + 1) * P)
                    starts = first and k == 0 and (t == 0 or pitch == BLK)
                    mm(o, hi[:, kt, x], w_hi[slot][:, c:c + width], start=starts, stop=False, skip_group_check=True)
                    mm(o, hi[:, kt, x], w_lo[slot][:, c:c + width], start=False, stop=False, skip_group_check=True)
                    last = mm(o, lo[:, kt, x], w_hi[slot][:, c:c + width], start=False, stop=True, skip_group_check=True)
            return last

        def chunk(at, j, wait, emit):
            pe.wait_ge(lo_ready, at.at(j) + 1)
            if wait:
                pe.wait_ge(*wait)
            emit().then_inc(chunks_done, 1)

        def gemm(at, number, the_set, n=NB, ready=None, hi=x_hi, lo=x_lo, same=False, tokenwise=False, steps=None):
            await_set(number, same)
            out = sets[the_set]
            for j in range(n):
                kts = (2 * j, 2 * j + 1)
                wait = ready(kts[1]) if ready else None
                if tokenwise:
                    chunk(at, j, wait, lambda: tokens(at, j, out, hi, lo, kts, j == 0, BLK))
                else:
                    chunk(at, j, wait, lambda: features(at, j, out, hi, lo, kts, j == 0))
                if steps and j in steps:
                    steps[j]()

        def narrow(at, out, width):
            pe.wait_ge(lo_ready, at.at(0) + 1)
            s, o = at.slot(0), out[0:width, 0:S]
            for kt in range(KT):
                c = slice(kt * width, (kt + 1) * width)
                mm(o, w_hi[s][:, c], x_hi[:, kt, :], start=kt == 0, stop=False)
                mm(o, w_hi[s][:, c], x_lo[:, kt, :], start=False, stop=False)
                last = mm(o, w_lo[s][:, c], x_hi[:, kt, :], start=False, stop=kt == KT - 1)
            last.then_inc(chunks_done, 1)

        def operand_ready(count):
            return lambda kt: (x_ready, count + kt + 1)

        pe.wait_ge(ones_ready, 1)
        for _ in range(WARM_UP):
            mm(m[3][:, 0:P], ones[:, :], ones[:, :], start=True, stop=True)

        def relative():
            pe.wait_ge(small_in, 80)
            pe.wait_ge(consts, 1)
            mm(m[3][0:HEADS, :], rel[:, :], ohd[:, :], start=True, stop=True).then_inc(rel_done, 1)

        def stats(k, bank, count):
            pe.wait_ge(stats_ready, count)
            mm(m[bank][:, 0:S], ones[:, :], stat[:, k, :], start=True, stop=True)
            for t in range(TT):
                last = mm(m[bank][:, S + t:S + t + 1], stat[:, k, t * P:(t + 1) * P], ones[:, 0:1], start=True, stop=True)
            last.then_inc(stats_sum, 1)

        for n in range(4):
            gemm(Pos(C_KV + n * NB), B_KV + n, n % 2, ready=operand_ready(0) if n == 0 else None,
                 steps={1: relative, 6: lambda: stats(0, 0, 4)} if n == 0 else None)
        for n in range(4, 6):
            gemm(Pos(C_KV + n * NB), B_KV + n, n % 2, tokenwise=True)
        await_set(B_G1)
        narrow(Pos(C_G1), sets[B_G1 % 2], 3 * HEADS)

        def gates():
            pe.wait_ge(gates_sig, 1)
            for t in range(TT):
                last = nc.tensor.transpose(m[0][:, t * 48:(t + 1) * 48], g_sig[:, (1 - t) * P:(2 - t) * P],
                                           ident[0:3 * HEADS, 0:3 * HEADS])
            last.then_inc(gates_done, 1)

        for n in range(2):
            await_set(B_CMP + n)
            out = sets[(B_CMP + n) % 2][0:GROUPS * NC, 0:CH]
            at = Pos(C_CMP + n * NB)
            pe.wait_ge(blk_ready, n + 1)
            for j in range(NB):
                pe.wait_ge(lo_ready, at.at(j) + 1)
                s = at.slot(j)
                for k in range(4):
                    kt, c = 4 * j + k, slice(k * CH, (k + 1) * CH)
                    mm(out, blk_hi[:, n, kt, :], w_hi[s][:, c], start=kt == 0, stop=False)
                    mm(out, blk_hi[:, n, kt, :], w_lo[s][:, c], start=False, stop=False)
                    last = mm(out, blk_lo[:, n, kt, :], w_hi[s][:, c], start=False, stop=kt == CB - 1)
                last.then_inc(chunks_done, 1)
                if n == 0 and j == 3:
                    gates()

        def hidden():
            pe.wait_ge(hid_ready, 2)
            for n in range(2):
                for f in range(2):
                    o = (n * 2 + f) * GROUPS * NC
                    last = nc.tensor.transpose(m[2][:, o:o + GROUPS * NC], hid_in[:, n, f * P:(f + 1) * P],
                                               ident[0:GROUPS * NC, 0:GROUPS * NC])
            last.then_inc(hid_done, 1)

        def compressed():
            pe.wait_ge(hid_copied, 1)
            for f in range(2):
                mm(m[0][:, 0:GROUPS * NC], w2[:, 0, f, :], hid[:, 0, f, :], start=f == 0, stop=f == 1)
            for gr in range(GROUPS):
                for f in range(2):
                    last = mm(m[1][0:NC, gr * DH:(gr + 1) * DH], hid[:, 1, f, gr * NC:(gr + 1) * NC], w2[:, 1, f, :],
                              start=f == 0, stop=f == 1)
            last.then_inc(kvc_sum, 1)

        def scores(gi, n):
            if n == 0:
                pe.wait_ge(taken, gi + (B_Q + 1))
            if real(gi, n - 1):
                pe.wait_ge(masked, gi * HPG + n)
            if real(gi, n - 3):
                pe.wait_ge(o_ready, gi * HPG + (n - 2))
            q0, q1 = q_t[:, n, P:S], q_t[:, n, 0:P]
            mm(m[0][:, 0:P], q0, k_sw[:, 0, gi, 0:P], start=True, stop=True)
            mm(m[0][:, P:TRI], q1, k_sw[:, 0, gi, :], start=True, stop=True)
            mm(m[0][:, TRI:TRI + NC], q0, k_c[:, gi, :], start=True, stop=True)
            mm(m[0][:, TRI + 16:TRI + 16 + NC], q1, k_c[:, gi, :], start=True, stop=True)
            mm(m[1][:, 0:P], q0, k_sw[:, 1, gi, 0:P], start=True, stop=True)
            mm(m[1][:, P:TRI], q1, k_sw[:, 1, gi, :], start=True, stop=True).then_inc(scores_done, 1)

        def transposes(gi, n):
            pe.wait_ge(probs_ready, gi * HPG + (n + 1))
            if real(gi, n - 1):
                pe.wait_ge(pt_ready, gi * HPG + n)
            pr = prob[n % 2]
            tr = nc.tensor.transpose
            for b, o in ((2, O_SEL), (3, O_WIN)):
                for k in range(3):
                    tr(m[b][:, k * P:(k + 1) * P], pr[:, o + k * P:o + (k + 1) * P], ident[:, :])
            tr(m[2][0:NC, TRI:BLK], pr[:, O_CMP:O_CMP + NC], ident[:, :])
            tr(m[3][0:NC, TRI:BLK], pr[:, O_CMP + 16:O_CMP + 16 + NC], ident[:, :]).then_inc(pt_done, 1)

        def values(gi, n):
            if n == 0:
                pe.wait_ge(vg_ready, gi + 1)
            pe.wait_ge(pt_ready, gi * HPG + (n + 1))
            if n + 2 < HPG:
                pe.wait_ge(masked, gi * HPG + (n + 3))
            if real(gi, n - 1):
                pe.wait_ge(o_ready, gi * HPG + n)
            for b in range(2):
                mm(m[1][:, 0:S], v_g[:, b, 0, :], prob_t[:, b, 0:S], start=b == 0, stop=False)
                mm(m[1][:, P:S], v_g[:, b, 1, :], prob_t[:, b, S:TRI], start=False, stop=False)
            mm(m[1][:, 0:S], v_cg[:, :], prob_ct[:, :], start=False, stop=True).then_inc(o_done, 1)

        def attention(gi, slot):
            n = slot // 2
            if slot % 2 == 0:
                if n < HPG:
                    scores(gi, n)
            else:
                if real(gi, n - 2):
                    values(gi, n - 2)
                if real(gi, n - 1):
                    transposes(gi, n - 1)

        def attentions(gi, slots=NB):
            return {s: lambda s=s: attention(gi, s) for s in range(slots)}

        gemm(Pos(C_Q), B_Q, B_Q % 2, steps={2: hidden, 4: compressed})
        gemm(Pos(C_Q + NB), B_Q + 1, (B_Q + 1) % 2, steps=attentions(0))
        with pe.Fori(1, GROUPS - 1) as gi:
            gemm(Pos(C_Q + NB, gi, NB), gi + (B_Q + 1), (B_Q + 1) % 2, same=True, steps=attentions(gi))

        def heads_ready(kt):
            return (o_ready, kt + 1)

        await_set(B_OUT)
        at, slot = Pos(C_OUT), 0
        for block_no, j0, count in ((0, 0, 6), (1, 0, 6), (0, 6, 2), (1, 6, 2)):
            for j in range(j0, j0 + count):
                kts = (2 * j, 2 * j + 1)
                if (block_no, j) == (1, 0):
                    await_set(B_OUT + 1)
                chunk(at, slot, heads_ready(kts[1]),
                      lambda: features(at, slot, sets[(B_OUT + block_no) % 2], o_hi, o_lo, kts, j == 0))
                if slot < ATT_SLOTS:
                    attention(3, slot)
                slot += 1
        for n in (2, 3):
            gemm(Pos(C_OUT, n, NB), B_OUT + n, (B_OUT + n) % 2, hi=o_hi, lo=o_lo)

        def up(i, first):
            gemm(Pos(C_UP, i, 2 * NB), i * 2 + B_UP, B_UP % 2, ready=operand_ready(KT) if first else None,
                 steps={3: lambda: stats(0, 0, 8)} if first else None)
            gemm(Pos(C_UP + NB, i, 2 * NB), i * 2 + (B_UP + 1), (B_UP + 1) % 2)

        up(0, True)
        with pe.Fori(1, NUP) as i:
            up(i, False)
        with pe.Fori(0, 2) as i:
            for b in range(2):
                gemm(Pos(C_DOWN + b * ND, i, 2 * ND), i * 2 + (B_DOWN + b), (B_DOWN + b) % 2, n=ND,
                     hi=f_hi, lo=f_lo, ready=(lambda kt: (f_ready, kt // FT + 1)) if b == 0 else None)

        def mlstm(i, first):
            at, number = ml_block(i, 0)
            out = sets[ml_set(i, 0)]
            await_set(number)
            for j in range(NB):
                kts = (2 * j, 2 * j + 1)

                def pool_chunk():
                    tokens(at, j, out, x_hi, x_lo, kts, j == 0, PG, pitch=PG)
                    return features(at, j, out, x_hi, x_lo, kts, j == 0, ft=2, ft0=2)

                chunk(at, j, (x_ready, 2 * KT + kts[1] + 1) if first else None, pool_chunk)
                if first and j == 5:
                    stats(0, 0, 16)
                    stats(1, 1, 16)
            if first:
                await_set(B_ML + 1)
                narrow(Pos(C_ML + NB), sets[(B_ML + 1) % 2], 2 * MH)

            def gate_inputs():
                pe.wait_ge(taken, B_ML + 2)
                for t in range(TT):
                    last = nc.tensor.transpose(m[3][:, t * 2 * MH:(t + 1) * 2 * MH], g_fm[:, t * P:(t + 1) * P],
                                               ident[0:2 * MH, 0:2 * MH])
                last.then_inc(gt_done, 1)

            def pooled():
                pe.wait_ge(taken, number + 1)
                pe.wait_ge(cur_in, i * 16 + 16)
                if not first:
                    pe.wait_ge(mp_ready, i * 2)
                for c in range(2):
                    for s in range(TT):
                        last = mm(m[0][:, c * S + s * P:(c + 1) * S], t1[:, s, c * P:(c + 1) * P],
                                  cur[:, P_BAND + s * (S + P):P_BAND + (s + 1) * S], start=s == 0, stop=s == 1)
                last.then_inc(pool_done, 1)

            def mixed():
                pe.wait_ge(pool_ready, i + 1)
                if not first:
                    pe.wait_ge(mpt_ready, i * 2)
                for o in range(2):
                    for c in range(2):
                        w = P_W + c * PG + o * P
                        last = mm(m[1][:, o * S:(o + 1) * S], cur[:, w:w + P], t2[:, c, :], start=c == 0, stop=c == 1)
                last.then_inc(mix_done, 1)

            def forget_sums():
                pe.wait_ge(g2_f, 1)
                mm(m[3][:, 0:MH], tri, g_t[:, 0, 0, :], start=True, stop=True)
                mm(m[3][:, MH:2 * MH], ones[:, :], g_t[:, 0, 0, :], start=True, stop=False)
                mm(m[3][:, MH:2 * MH], tri, g_t[:, 0, 1, :], start=False, stop=True).then_inc(f_done, 1)

            def g_rows():
                pe.wait_ge(g_ready, 1)
                for t in range(TT):
                    last = nc.tensor.transpose(m[2][0:MH, t * P:(t + 1) * P], g_t[:, 2, t, :], ident[:, :])
                last.then_inc(g_row_done, 1)

            def g_broadcast():
                pe.wait_ge(g_row_ready, 1)
                pe.wait_ge(yb_made, 1)
                for k in range(MH):
                    last = mm(m[k // 2][:, (k % 2) * S:(k % 2 + 1) * S], sel[:, k * P:(k + 1) * P], g_row,
                              start=True, stop=True)
                last.then_inc(g_bc_done, 1)

            gemm(ml_block(i, 1)[0], ml_block(i, 1)[1], ml_set(i, 1), 
                 steps={1: pooled, 3: mixed} | ({0: gate_inputs, 4: forget_sums, 5: g_rows} if first else {}))
            gemm(ml_block(i, 2)[0], ml_block(i, 2)[1], ml_set(i, 2), steps={0: g_broadcast} if first else None)
            gemm(ml_block(i, 3)[0], ml_block(i, 3)[1], ml_set(i, 3), tokenwise=True)

            def head_scores(n):
                pe.wait_ge(qkv_ready, i * 2 + 2)
                if first and n == 0:
                    pe.wait_ge(decay_arg, 1)
                if not (first and n == 0):
                    pe.wait_ge(mp_ready, i * 2 + n)
                if n == 0:
                    pe.wait_ge(yb_made, i + 1)
                for t in range(TT):
                    for k in range(2):
                        last = mm(m[0][:, t * P:(t + 1) * P + t * P], qm[:, 2 * n + k, t * P:(t + 1) * P],
                                  km[:, 2 * n + k, 0:(t + 1) * P], start=k == 0, stop=k == 1)
                last.then_inc(ms_done, 1)

            def head_transposes(n):
                pe.wait_ge(mp_ready, i * 2 + (n + 1))
                if not (first and n == 0):
                    pe.wait_ge(mpt_ready, i * 2 + n)
                for k in range(3):
                    last = nc.tensor.transpose(m[1][:, k * P:(k + 1) * P], pm[:, k * P:(k + 1) * P], ident[:, :])
                last.then_inc(mpt_done, 1)

            def head_values(n):
                pe.wait_ge(mpt_ready, i * 2 + (n + 1))
                if n == 0:
                    pe.wait_ge(taken, ml_block(i, 3)[1] + 1)
                if not (first and n == 0):
                    pe.wait_ge(mh_ready, i * 2 + n)
                for f in range(2):
                    c = n * MD + f * P
                    mm(m[2][:, f * S:(f + 1) * S], vm[:, 0, c:c + P], pm_t[:, 0:S], start=True, stop=False)
                    last = mm(m[2][:, f * S + P:(f + 1) * S], vm[:, 1, c:c + P], pm_t[:, S:TRI], start=False, stop=True)
                last.then_inc(mh_done, 1)

            def head_squares(n):
                pe.wait_ge(mh_sum, i * 2 + (n + 1))
                if not (first and n == 0):
                    pe.wait_ge(mn_var, i * 2 + n)
                mm(m[3][:, 0:S], ones[:, :], t2[:, 2 * n, :], start=True, stop=True).then_inc(mn_done, 1)

            gemm(ml_block(i, 4)[0], ml_block(i, 4)[1], ml_set(i, 4),
                 steps={1: lambda: head_scores(0), 3: lambda: head_transposes(0), 4: lambda: head_values(0),
                        5: lambda: head_scores(1), 7: lambda: head_transposes(1)})
            gemm(ml_block(i, 5)[0], ml_block(i, 5)[1], ml_set(i, 5),
                 steps={1: lambda: head_values(1), 2: lambda: head_squares(0), 5: lambda: head_squares(1)})

        mlstm(0, True)
        with pe.Fori(1, 4) as i:
            mlstm(i, False)

        with pe.Fori(0, 4) as i:
            gemm(Pos(C_MG, i, NMG), i * 4 + B_MG, B_MG % 2)
            gemm(Pos(C_MG + NB, i, NMG), i * 4 + (B_MG + 1), (B_MG + 1) % 2)
            gemm(Pos(C_MG + 2 * NB, i, NMG), i * 4 + (B_MG + 2), B_MG % 2, hi=ya_hi, lo=ya_lo,
                 ready=lambda kt: (ya_ready, kt // FT + 1))
            gemm(Pos(C_MG + 3 * NB, i, NMG), i * 4 + (B_MG + 3), (B_MG + 1) % 2, n=NB // 2, hi=yb_hi, lo=yb_lo,
                 ready=lambda kt: (yb_ready, kt // 2 + 1))
        with pe.Fori(0, 2) as i:
            for b in range(2):
                gemm(Pos(C_WO + b * NB, i, 2 * NB), i * 2 + (B_WO + b), (B_WO + b) % 2, hi=m_hi, lo=m_lo,
                     ready=(lambda kt: (m_ready, kt // FT + 1)) if b == 0 else None)
        pe.wait_ge(stats_ready, 19)
        mm(m[0][:, 0:S], ones[:, :], stat[:, 0, :], start=True, stop=False)
        for f in range(FT):
            pe.wait_ge(out_sq, f // 2 + 1)
            last = mm(m[0][:, 0:S], ones[:, :], sq[:, f, :], start=False, stop=f == FT - 1)
        last.then_inc(stats_sum, 1)

    ctx.close()


def bucket(n):
    exact = BUCKETS // 2
    if n < exact:
        return n
    large = np.log(np.float32(n) / np.float32(exact)) / np.float32(math.log(MAX_DIST / exact))
    return min(exact + int(np.float32(large) * np.float32(BUCKETS - exact)), BUCKETS - 1)


def shape_constants():
    ohd = np.zeros((BUCKETS + 1, 2 * S), np.float32)
    for i in range(2 * S):
        if i < S:
            ohd[bucket(S - 1 - i), i] = 1
        else:
            ohd[BUCKETS, i] = NEG
    t = np.arange(S).reshape(TT, P).T
    valid = (t[::-1] >= CB - 1).astype(np.float32)
    p = np.arange(P)
    causal = np.zeros((P, TRI), np.float32)
    causal[:, 0:P] = np.where(p[None, :] <= p[:, None], 0, NEG)
    causal[:, P:] = np.where(np.arange(S)[None, :] <= p[:, None] + P, 0, NEG)
    tri = (p[:, None] <= p[None, :]).astype(np.float32)
    sel = np.zeros((MH, MH, P), np.float32)
    for k in range(MH):
        sel[k, k] = 1
    band = np.zeros((len(POOLS), S, S), np.float32)
    for n, w in enumerate(POOLS):
        for t_ in range(S):
            lo = max(t_ + 1 - w, 0)
            band[n, lo:t_ + 1, t_] = np.float32(1) / np.float32(t_ + 1 - lo)
            band[n, t_, t_] -= 1
    return {"ohd": ohd, "valid": valid, "causal": causal, "tri": tri,
            "sel": sel.reshape(MH, MH * P)}, band


def blocks(w):
    k, n = w.shape
    return w.reshape(k // (2 * P), 2, P, n // BLK, BLK).transpose(3, 0, 2, 1, 4).reshape(n // BLK, k // (2 * P), P, CC)


def lay_out(a):
    def vec(x):
        return x.reshape(-1, P).T

    w_in = a["nsa_w_in"][0]
    kvw = HEADS * DH
    k_width = GROUPS * DH
    part = [w_in[:, kvw + n * k_width:kvw + (n + 1) * k_width] for n in range(6)]
    stream = [blocks(part[n])[0] for n in (0, 1, 2, 4, 3, 5)]

    def gate_chunk(w):
        out = np.zeros((1, P, CC), np.float32)
        out[0, :, :KT * w.shape[1]] = w.reshape(KT, P, w.shape[1]).transpose(1, 0, 2).reshape(P, -1)
        return out

    stream.append(gate_chunk(w_in[:, kvw + 6 * k_width:]))
    for name in ("cmp_w1_k", "cmp_w1_v"):
        stream.append(a[name][0].reshape(NB, 4, P, CH).transpose(0, 2, 1, 3).reshape(NB, P, CC))
    stream += list(blocks(w_in[:, :kvw]))
    o = blocks(a["nsa_w_out"][0])
    stream += [o[0][:6], o[1][:6], o[0][6:], o[1][6:], o[2], o[3]]
    up = a["ffn_w_in"][0]
    gate_part, value_part = blocks(up[:, :FF]), blocks(up[:, FF:])
    for j in range(NUP):
        stream += [gate_part[j], value_part[j]]
    stream += list(blocks(a["ffn_w_out"][0]))

    w2 = a["w_in_2"][0]
    at = 0
    cols = {}
    for name, width in (("q", D), ("k", D), ("v", D), ("o", D), ("z", D), ("gates", 2 * MH), ("u", len(POOLS) * PG),
                        ("zb", len(POOLS) * PG), ("ga", D), ("gb", D)):
        cols[name] = w2[:, at:at + width]
        at += width
    big = {n: blocks(cols[n]) for n in ("q", "k", "v", "o", "z", "ga", "gb")}
    for i in range(4):
        uz = np.concatenate([cols["u"][:, i * PG:(i + 1) * PG], cols["zb"][:, i * PG:(i + 1) * PG]], axis=1)
        stream.append(blocks(uz)[0])
        if i == 0:
            stream.append(gate_chunk(cols["gates"]))
        stream += [big[n][i] for n in ("q", "k", "v", "o", "z")]
    pa, pb = blocks(a["w_proj_mlstm_2"][0]), blocks(a["w_proj_pool_2"][0])
    for i in range(4):
        stream += [big["ga"][i], big["gb"][i], pa[i], pb[i]]
    stream += list(blocks(a["w_out_2"][0]))

    constants, band = shape_constants()
    conv_w, conv_b = a["qk_conv_w_2"][0], a["qk_conv_b_2"][0]
    conv = np.concatenate([conv_w, conv_b[None]], axis=0).reshape(5, 2, 4, FT, P)
    cur = np.concatenate([
        conv.transpose(2, 4, 1, 3, 0).reshape(4, P, 2 * FT * 5),
        a["mlstm_norm_w_2"][0].reshape(4, FT, P).transpose(0, 2, 1),
        a["pool_scale_2"][0].reshape(4, 2, P).transpose(0, 2, 1),
        a["pool_w_2"][0].reshape(4, 2, P, PG).transpose(0, 2, 1, 3).reshape(4, P, 2 * PG),
        band.reshape(4, TT, P, S).transpose(0, 2, 1, 3).reshape(4, P, TT * S),
    ], axis=2)
    return {
        "x": a["x"][0].T.reshape(KT, P, S),
        "weights": np.concatenate(stream, axis=0),
        "gains": np.stack([vec(a["mix_norm_g"][0]), vec(a["ffn_norm_g"][0]), vec(a["final_norm_g"]),
                           vec(a["norm_pre_w_2"][0]), vec(a["norm_post_w_2"][0])], axis=1),
        "rel": a["rel_bias"],
        "w2": np.stack([a["cmp_w2_k"][0].reshape(2, P, DH), a["cmp_w2_v"][0].reshape(2, P, DH)]).transpose(2, 0, 1, 3),
        "pos": np.stack([a["cmp_pos_k"][0].T, a["cmp_pos_v"][0].T], axis=1),
        "g_bias": np.broadcast_to(np.concatenate([a["mlstm_i_bias_2"][0], a["mlstm_f_bias_2"][0]]), (P, 2 * MH)),
        "cur": cur,
        **constants,
    }


def kernel(**inputs):
    import concourse.bacc as bacc
    from concourse.bass_utils import run_bass_kernel_spmd

    nc = bacc.Bacc("TRN2", target_bir_lowering=False, num_devices=1)
    arrays = {f"in_{k}": np.ascontiguousarray(v) for k, v in lay_out({k: np.asarray(v) for k, v in inputs.items()}).items()}
    d = {k[3:]: nc.dram_tensor(k, v.shape, mybir.dt.from_np(v.dtype), kind="ExternalInput").ap() for k, v in arrays.items()}
    d["out"] = nc.dram_tensor("out", (KT, P, S), F32, kind="ExternalOutput").ap()
    program(nc, d)
    r = run_bass_kernel_spmd(nc, [arrays], core_ids=[0])
    return r.results[0]["out"].reshape(D, S).T.reshape(1, S, D)
```
